# Optimizing a Trainium2 kernel written in Bass

```python
import jax, jax.numpy as jnp
from jax import lax
import numpy as np

D_MODEL = 1024
BATCH = 1
SEQ = 512
DEPTH = 2

CHUNK = 64
D_MIX = D_MODEL
N_Q_HEADS = 8
N_KV_HEADS = 2
HEAD_DIM = 64
D_ATTN = N_Q_HEADS * HEAD_DIM
D_KV = N_KV_HEADS * HEAD_DIM
WINDOW = 128
WINDOW_CHUNKS = WINDOW // CHUNK
D_CONV = D_MIX // 4
CONV_WIDTH = 31
D_SC = D_MIX // 4
SC_WIDTH = 3
N_IN = D_ATTN + 2 * D_KV + 2 * D_CONV + 3 * D_SC
D_FF = 2816
RMS_EPS = 1e-6
LN_EPS = 1e-5
NEG_INF = -1e30

kernel_name = "hybrid_conformer_shortconv_swa_sink_encoder"

def rms_normalize(x, eps=RMS_EPS):
    xf = x.astype(jnp.float32)
    return xf * lax.rsqrt(jnp.mean(xf * xf, axis=-1, keepdims=True) + eps)

def rmsnorm(x, g):
    return (rms_normalize(x) * g.astype(jnp.float32)).astype(x.dtype)

def layernorm(x, g, b):
    xf = x.astype(jnp.float32)
    mu = jnp.mean(xf, axis=-1, keepdims=True)
    var = jnp.mean(jnp.square(xf - mu), axis=-1, keepdims=True)
    y = (xf - mu) * lax.rsqrt(var + LN_EPS) * g.astype(jnp.float32) + b.astype(jnp.float32)
    return y.astype(x.dtype)

def causal_dwconv(x, w):
    k = w.shape[0]
    return lax.conv_general_dilated(
        x, w[:, None, :].astype(x.dtype), window_strides=(1,), padding=[(k - 1, 0)],
        dimension_numbers=("NWC", "WIO", "NWC"), feature_group_count=x.shape[-1])

def swiglu(x, w_gate, w_up, w_down):
    return (jax.nn.silu(x @ w_gate) * (x @ w_up)) @ w_down

def window_chunks(a):
    nc = a.shape[1]
    pad = [(0, 0)] * a.ndim
    pad[1] = (WINDOW_CHUNKS - 1, 0)
    ap = jnp.pad(a, pad)
    parts = [ap[:, j:j + nc] for j in range(WINDOW_CHUNKS)]
    return jnp.concatenate(parts, axis=2)

def swa_sink_attention(q, k, v, sink):
    b, t, _ = q.shape
    nc = t // CHUNK
    grp = N_Q_HEADS // N_KV_HEADS
    qc = q.reshape(b, nc, CHUNK, N_KV_HEADS, grp, HEAD_DIM)
    kw = window_chunks(k.reshape(b, nc, CHUNK, N_KV_HEADS, HEAD_DIM))
    vw = window_chunks(v.reshape(b, nc, CHUNK, N_KV_HEADS, HEAD_DIM))
    s = jnp.einsum('bnqkgd,bnskd->bnkgqs', qc, kw).astype(jnp.float32) * (HEAD_DIM ** -0.5)
    chunk_idx = jnp.arange(nc)[:, None] - jnp.arange(WINDOW_CHUNKS - 1, -1, -1)[None, :]
    valid = jnp.repeat(chunk_idx >= 0, CHUNK, axis=1)
    s = jnp.where(valid[None, :, None, None, None, :], s, NEG_INF)
    sk = sink.astype(jnp.float32).reshape(N_KV_HEADS, grp)[None, None, :, :, None, None]
    m = jnp.maximum(jnp.max(s, axis=-1, keepdims=True), sk)
    e = jnp.exp(s - m)
    p = e / (jnp.sum(e, axis=-1, keepdims=True) + jnp.exp(sk - m))
    o = jnp.einsum('bnkgqs,bnskd->bnqkgd', p.astype(v.dtype), vw)
    return o.reshape(b, t, D_ATTN)

def setup_inputs(seed: int = 0) -> dict:
    key = jax.random.key(seed)
    ks = jax.random.split(key, 16)
    nrm = jax.random.normal
    f32 = jnp.float32
    x = nrm(ks[0], (BATCH, SEQ, D_MODEL), f32)
    g_norm = 1.0 + 0.02 * nrm(ks[1], (DEPTH, 3, D_MODEL), f32)
    w_ff_gate = nrm(ks[2], (DEPTH, 2, D_MODEL, D_FF), f32) * D_MODEL ** -0.5
    w_ff_up = nrm(ks[3], (DEPTH, 2, D_MODEL, D_FF), f32) * D_MODEL ** -0.5
    w_ff_down = nrm(ks[4], (DEPTH, 2, D_FF, D_MODEL), f32) * D_FF ** -0.5
    w_in = nrm(ks[5], (DEPTH, D_MODEL, N_IN), f32) * D_MODEL ** -0.5
    w_dw31 = nrm(ks[6], (DEPTH, CONV_WIDTH, D_CONV), f32) * CONV_WIDTH ** -0.5
    b_dw31 = 0.02 * nrm(ks[7], (DEPTH, D_CONV), f32)
    g_ln_conv = 1.0 + 0.02 * nrm(ks[8], (DEPTH, D_CONV), f32)
    b_ln_conv = 0.02 * nrm(ks[9], (DEPTH, D_CONV), f32)
    w_sc3 = nrm(ks[10], (DEPTH, SC_WIDTH, D_SC), f32) * SC_WIDTH ** -0.5
    sinks = 0.5 * nrm(ks[11], (DEPTH, N_Q_HEADS), f32)
    g_grp = 1.0 + 0.02 * nrm(ks[12], (DEPTH, D_MIX), f32)
    w_out = nrm(ks[13], (DEPTH, D_MIX, D_MODEL), f32) * D_MIX ** -0.5
    g_final = 1.0 + 0.02 * nrm(ks[14], (D_MODEL,), f32)
    return {"x": x, "g_norm": g_norm, "w_ff_gate": w_ff_gate, "w_ff_up": w_ff_up,
            "w_ff_down": w_ff_down, "w_in": w_in, "w_dw31": w_dw31, "b_dw31": b_dw31,
            "g_ln_conv": g_ln_conv, "b_ln_conv": b_ln_conv, "w_sc3": w_sc3, "sinks": sinks,
            "g_grp": g_grp, "w_out": w_out, "g_final": g_final}

def reference(x, g_norm, w_ff_gate, w_ff_up, w_ff_down, w_in, w_dw31, b_dw31,
              g_ln_conv, b_ln_conv, w_sc3, sinks, g_grp, w_out, g_final):
    o_q = 0
    o_k = o_q + D_ATTN
    o_v = o_k + D_KV
    o_ca = o_v + D_KV
    o_cg = o_ca + D_CONV
    o_sb = o_cg + D_CONV
    o_sc = o_sb + D_SC
    o_sx = o_sc + D_SC
    for i in range(DEPTH):
        h = rmsnorm(x, g_norm[i, 0])
        x = x + 0.5 * swiglu(h, w_ff_gate[i, 0], w_ff_up[i, 0], w_ff_down[i, 0])

        h = rmsnorm(x, g_norm[i, 1])
        u = h @ w_in[i]
        y_attn = swa_sink_attention(u[..., o_q:o_k], u[..., o_k:o_v], u[..., o_v:o_ca], sinks[i])
        z = u[..., o_ca:o_cg] * jax.nn.sigmoid(u[..., o_cg:o_sb])
        z = causal_dwconv(z, w_dw31[i]) + b_dw31[i]
        y_conv = jax.nn.silu(layernorm(z, g_ln_conv[i], b_ln_conv[i]))
        y_sc = u[..., o_sb:o_sc] * causal_dwconv(u[..., o_sc:o_sx] * u[..., o_sx:], w_sc3[i])
        y = jnp.concatenate([rms_normalize(y_attn), rms_normalize(y_conv), rms_normalize(y_sc)], axis=-1)
        y = (y * g_grp[i].astype(jnp.float32)).astype(x.dtype)
        x = x + y @ w_out[i]

        h = rmsnorm(x, g_norm[i, 2])
        x = x + 0.5 * swiglu(h, w_ff_gate[i, 1], w_ff_up[i, 1], w_ff_down[i, 1])
    return rmsnorm(x, g_final)


_drawn_inputs = setup_inputs


def setup_inputs(seed=0):
    import zlib

    import numpy as np

    out = dict(_drawn_inputs(seed))
    spreads = {}
    factors = {'g_ln_conv': 4.74, 'b_ln_conv': 4.794, 'sinks': 8.0, 'g_grp': 2.827, 'g_final': 2.886}
    for name, (base, spread) in spreads.items():
        noise = np.random.default_rng([zlib.crc32(name.encode()), seed]).standard_normal(out[name].shape)
        drawn = base * np.exp(spread * noise) if base else spread * noise
        out[name] = __import__('jax').numpy.asarray(drawn.astype(out[name].dtype))
    for name, factor in factors.items():
        out[name] = (out[name] * factor).astype(out[name].dtype)
    return out
```

```python
from contextlib import ExitStack

import concourse.bass as bass
from concourse import mybir

F32 = mybir.dt.float32
F32R = mybir.dt.float32r
ALU = mybir.AluOpType
ACT = mybir.ActivationFunctionType
AX = mybir.AxisListType

P = 128
RMS_EPS = 1e-6
LN_EPS = 1e-5
CHUNK = 64
HEADS, KV_HEADS, HEAD_DIM = 8, 2, 64

RAW = 2
RING = 4


def encoder_trunk(nc, x_in, g_norm, w_gate, w_up, w_down, w_in, w_dw31, b_dw31, g_ln, b_ln, w_sc3,
                  sinks, g_grp, w_out, g_final, out):
    _, T, D = x_in.shape
    L, _, _, FF = w_gate.shape
    N_IN = w_in.shape[2]
    KD = D // P
    FT = FF // P
    HALF = FT // 2
    NT = T // P
    UT = N_IN // P
    TAPS = w_dw31.shape[1]
    SC_TAPS = w_sc3.shape[1]
    D_ATTN = HEADS * HEAD_DIM
    D_CONV = w_dw31.shape[2]
    CT = D_CONV // P
    assert (KD, NT, UT, CT) == (8, 4, 16, 2) and T == 512 and FT % 2 == 0 and D_ATTN == 4 * P

    CA, CG, UK, UV, UQ, SB, SC, SX = [0, 2], [1, 3], 4, 5, 6, 10, 12, 14
    COL = D_ATTN + 2 * KV_HEADS * HEAD_DIM
    COLS = ([COL, COL + 2 * P, COL + P, COL + 3 * P, D_ATTN, D_ATTN + P] + [None] * 4
            + [COL + (4 + i) * P for i in range(6)])

    GATE_UP, DOWN, W_IN, W_OUT = 0, 2 * FT, 2 * FT + 2 * KD, 2 * FT + 2 * KD + UT
    FFN = [0, W_OUT + KD]
    UNITS = FFN[1] + 2 * FT + 2 * KD
    PROJ = [0, 2 * FT, 2 * FT + UT]
    PROJS = PROJ[2] + 2 * FT
    RES = [0, KD, 2 * KD]
    RESES = 3 * KD
    NORM_FFN0, NORM_MIX, NORM_ATTN, NORM_FFN1 = range(4)
    NORMS = 4
    NORM_LN, NORM_CONV, NORM_SC = range(3)
    NORMS_B = 3
    PAIRS = T // (2 * CHUNK)
    TAP_BLOCKS = [6, 6, 6, 4, 4, 4]
    assert sum(TAP_BLOCKS) == TAPS - 1

    C_NORM = 0
    C_GRP = C_NORM + 3 * L * KD + KD
    C_BDW = C_GRP + L * KD
    C_GLN = C_BDW + L * CT
    C_BLN = C_GLN + L * CT
    C_SC3 = C_BLN + L * CT
    N_PAR = C_SC3 + L * SC_TAPS * CT
    N_DW = L * TAPS * CT
    assert N_PAR <= P and N_DW <= P and UNITS % RING == 0

    with ExitStack() as ctx:
        def sb(name, shape, dt=F32):
            return ctx.enter_context(nc.sbuf_tensor(name, shape, dt))

        def sem(name):
            return ctx.enter_context(nc.semaphore(name))

        x = sb("x", [P, KD, T])
        xh = sb("xh", [P, KD, T], F32R)
        xl = sb("xl", [P, KD, T], F32R)
        raw = sb("raw", [P, RAW, HALF, P])
        wh = sb("wh", [P, RING, HALF, P], F32R)
        wl = sb("wl", [P, RING, HALF, P], F32R)
        sq = sb("sq", [P, 2, T])
        acc = sb("acc", [P, T])
        rstd = sb("rstd", [P, T])
        gate = sb("gate", [P, T])
        prod = sb("prod", [P, T])
        par = sb("par", [P, N_PAR])
        dw = sb("dw", [P, N_DW])
        ident = sb("ident", [P, P])
        ones = sb("ones", [P, P])
        rstd_b = sb("rstd_b", [P, T])
        sink = sb("sink", [P, L * KV_HEADS * 4])

        region = sb("region", [P, 2 * FT * T])
        offset = [0]

        def at(name, shape, dt=F32):
            size = 4
            for n in shape[1:]:
                size *= n
            t = nc.alloc_sbuf_tensor_at(name, shape, dt, offset=REGION + offset[0])
            offset[0] += size
            assert offset[0] <= 2 * FT * T * 4
            return t

        REGION = nc.sbuf_base - 2 * FT * T * 4
        acth = at("acth", [P, FT, T], F32R)
        actl = at("actl", [P, FT, T], F32R)
        offset[0] = 0
        u = at("u", [P, UT, T])
        uq = u[:, UQ:UQ + 4, :].rearrange("p j t -> p (j t)").rearrange("p (n j q) -> p n j q", j=4, q=CHUNK)
        yh = at("yh", [P, KD, T], F32R)
        yl = at("yl", [P, KD, T], F32R)
        z = at("z", [P, CT, TAPS - 1 + T + 2])
        cx = at("cx", [P, CT, SC_TAPS - 1 + T + 6])
        probs = at("probs", [P, 2, 4, P])
        probsT = at("probsT", [P, 2, 4, P])
        vtok = at("vtok", [P, 2 * PAIRS, P])
        soft = at("soft", [P, 8, PAIRS, 8])
        S_MAX, S_M, S_NEG, S_SINK, S_SUM, S_ES, S_DEN, S_R = range(8)
        offset[0] = 0
        xnat = at("xnat", [P, NT, D])
        parnat = at("parnat", [P, P])
        dwnat = at("dwnat", [P, P])
        sinknat = at("sinknat", [P, L * HEADS])
        offset[0] = 0
        yT = at("yT", [P, KD, T])
        ynat = at("ynat", [P, NT, D])

        bank = [ctx.enter_context(nc.psum_tensor(f"bank{i}", [P, T], F32)) for i in range(8)]
        RES_BANK, STAT, SCORES, PROBS_T, HEADS_OUT = 4, 6, 2, 4, 7

        raw_landed = [sem(f"raw_landed{i}") for i in range(RAW)]
        in_landed = [sem(f"in_landed{i}") for i in range(NT)]
        par_landed = sem("par_landed")
        out_landed = sem("out_landed")
        hi_ready = sem("hi_ready")
        lo_ready = sem("lo_ready")
        unit_done = sem("unit_done")
        proj_read = sem("proj_read")
        x_ready = sem("x_ready")
        xh_ready = sem("xh_ready")
        xl_ready = sem("xl_ready")
        sq_ready = sem("sq_ready")
        acc_ready = sem("acc_ready")
        stat_ready = sem("stat_ready")
        var_ready = sem("var_ready")
        root_ready = sem("root_ready")
        rstd_ready = sem("rstd_ready")
        gate_ready = sem("gate_ready")
        silu_ready = sem("silu_ready")
        prod_ready = sem("prod_ready")
        acth_ready = sem("acth_ready")
        actl_ready = sem("actl_ready")
        const_ready = sem("const_ready")
        ident_zero = sem("ident_zero")
        par_t = sem("par_t")
        in_t = sem("in_t")
        sinks_ready = sem("sinks_ready")
        sig_ready = sem("sig_ready")
        pads_zero = sem("pads_zero")
        conv_step = sem("conv_step")
        vec_step = sem("vec_step")
        mean_ready = sem("mean_ready")
        ln_ready = sem("ln_ready")
        silu_conv = sem("silu_conv")
        sc_ready = sem("sc_ready")
        sqb_ready = sem("sqb_ready")
        statb_ready = sem("statb_ready")
        varb_ready = sem("varb_ready")
        rootb_ready = sem("rootb_ready")
        rstdb_ready = sem("rstdb_ready")
        y_ready = sem("y_ready")
        yh_ready = sem("yh_ready")
        yl_ready = sem("yl_ready")
        v_t = sem("v_t")
        v_ready = sem("v_ready")
        scores_ready = sem("scores_ready")
        max_ready = sem("max_ready")
        exp_ready = sem("exp_ready")
        probs_ready = sem("probs_ready")
        probsT_ready = sem("probsT_ready")
        probsT_read = sem("probsT_read")
        o_ready = sem("o_ready")
        o_read = sem("o_read")
        sqa_ready = sem("sqa_ready")
        sqa_sum = sem("sqa_sum")
        passed = sem("passed")
        y_t = sem("y_t")
        y_scaled = sem("y_scaled")
        y_read = [sem("y_read_scalar"), sem("y_read_vector")]

        block = ctx.enter_context(nc.Block())

        def apart(eng):
            eng.sem_inc(passed, 1)

        gate_v = w_gate.rearrange("l j (k p) f -> l j p k f", p=P)
        up_v = w_up.rearrange("l j (k p) f -> l j p k f", p=P)
        down_v = w_down.rearrange("l j (h k p) c -> l j h p k c", p=P, h=2)
        in_v = w_in.rearrange("l (k p) c -> l p k c", p=P)
        out_attn_v = w_out[:, 0:D_ATTN, :].rearrange("l (h j p) c -> l h p j c", h=2, j=4)
        out_conv_v = w_out[:, D_ATTN:D, :].rearrange("l (g k p) c -> l g p k c", p=P, g=2)
        CONV_G, SC_G, ATTN_G = range(3)
        WO = [(CONV_G, 0, 4), (SC_G, 0, 4), (ATTN_G, 0, 2), (ATTN_G, 2, 2),
              (CONV_G, 4, 4), (SC_G, 4, 4), (ATTN_G, 4, 2), (ATTN_G, 6, 2)]
        GROUP_TILES = [[4, 5], [6, 7], [0, 1, 2, 3]]

        @block.sync
        def _(sp):
            def load(n, s, parts):
                sp.wait_ge(lo_ready, n + 1)
                apart(sp)
                for dst, src in parts:
                    sp.dma_start(dst, src).then_inc(raw_landed[s], 16)

            def ffn(l, j):
                with sp.Fori(0, FT) as f:
                    n = l * UNITS + FFN[j] + 2 * f
                    for s, v in enumerate((gate_v, up_v)):
                        load(n + s, s, [(raw[:, s, 0:KD, :], v[l, j, :, :, bass.ds(f * P, P)])])
                with sp.Fori(0, KD) as d:
                    n = l * UNITS + FFN[j] + DOWN + 2 * d
                    for s in range(2):
                        load(n + s, s, [(raw[:, s, :, :], down_v[l, j, s, :, :, bass.ds(d * P, P)])])

            with sp.Fori(0, L) as l:
                ffn(l, 0)
                for i in range(UT):
                    s = i % 2
                    dst = raw[:, s, 0:KD, :]
                    if COLS[i] is not None:
                        parts = [(dst, in_v[l, :, :, COLS[i]:COLS[i] + P])]
                    else:
                        j = i - UQ
                        parts = [(raw[:, s, 0:KD, h * 64:h * 64 + 64],
                                  in_v[l, :, :, (4 * h + j) * 64:(4 * h + j + 1) * 64]) for h in range(2)]
                    load(l * UNITS + W_IN + i, s, parts)
                for i, (g, d0, n) in enumerate(WO):
                    s = i % 2
                    c = slice(d0 * P, (d0 + n) * P)
                    if g == ATTN_G:
                        dst = raw[:, s, 0:KD, :].rearrange("p (j d) c -> p j (d c)", j=4)
                        parts = [(dst[64 * h:64 * h + 64], out_attn_v[l, h, :, :, c]) for h in range(2)]
                    else:
                        dst = raw[:, s, 0:KD, :].rearrange("p (k d) c -> p k (d c)", k=2)
                        parts = [(dst, out_conv_v[l, g, :, :, c])]
                    load(l * UNITS + W_OUT + i, s, parts)
                ffn(l, 1)
            for t in range(NT):
                for h in range(2):
                    sp.wait_ge(y_read[h], t + 1)
                sp.dma_start(out[0, t * P:(t + 1) * P, :], ynat[:, t, :]).then_inc(out_landed, 16)
            sp.wait_ge(out_landed, 16 * NT)

        def extra(n):
            more = [0, 0]
            for m in range(n % 2, n + 1, 2):
                if W_IN + UQ <= m < W_IN + UQ + 4:
                    more[m % 2] += 16
                if W_OUT <= m < W_OUT + KD and WO[m - W_OUT][0] == ATTN_G:
                    more[m % 2] += 16
            return more[n % 2]

        PER_SLOT = [16 * UNITS // 2 + extra(UNITS - 2 + s) for s in range(2)]

        @block.gpsimd
        def _(pool):
            nc.gpsimd.memset(ident[:, :], 0.0).then_inc(ident_zero, 1)
            nc.gpsimd.memset(ones[:, :], 1.0).then_inc(const_ready, 1)
            pool.wait_ge(ident_zero, 1)
            nc.gpsimd.affine_select(out=ident[:, :], in_=ident[:, :], compare_op=ALU.not_equal, fill=1.0,
                                    base=0, pattern=[[-1, P]], channel_multiplier=1).then_inc(const_ready, 1)

            def sum_squares(read, first, count=KD):
                for i in range(count):
                    pool.wait_ge(sq_ready, first + i + 1)
                    if i == 0:
                        if read is not None:
                            pool.wait_ge(stat_ready, read)
                            apart(pool)
                        nc.gpsimd.tensor_copy(acc[:, :], sq[:, i % 2, :]).then_inc(acc_ready, 1)
                    else:
                        pool.wait_ge(acc_ready, first + i)
                        nc.gpsimd.tensor_tensor(acc[:, :], acc[:, :], sq[:, i % 2, :], ALU.add)\
                            .then_inc(acc_ready, 1)

            sum_squares(None, 0)
            with nc.gpsimd.Fori(0, L) as l:
                r, n = KD + l * RESES, l * NORMS
                sum_squares(n + NORM_FFN0 + 1, r + RES[0])
                pool.wait_ge(x_ready, r + RES[1])
                apart(pool)
                nc.gpsimd.memset(z[:, :, 0:TAPS - 1], 0.0)
                nc.gpsimd.memset(cx[:, :, 0:SC_TAPS - 1], 0.0)
                nc.gpsimd.memset(probs[:, :, 0:2, CHUNK:P], 0.0).then_inc(pads_zero, 1)
                for p in range(PAIRS):
                    sqa = gate[:, :].rearrange("p (c j q) -> p j c q", c=2, j=4)
                    to = prod[:, p * P:(p + 1) * P].rearrange("p (c q) -> p c q", c=2)
                    pool.wait_ge(sqa_ready, l * PAIRS + p + 1)
                    for j in range(1, 4):
                        if j > 1:
                            pool.wait_ge(sqa_sum, l * 3 * PAIRS + 3 * p + j - 1)
                        nc.gpsimd.tensor_tensor(to, sqa[:, 0] if j == 1 else to, sqa[:, j], ALU.add)\
                            .then_inc(sqa_sum, 1)
                sum_squares(n + NORM_MIX + 1, r + RES[1])
                sum_squares(n + NORM_FFN1 + 1, r + RES[2])

        @block.scalar
        def _(act):
            for t in range(NT):
                act.dma_start(xnat[:, t, :], x_in[0, t * P:(t + 1) * P, :]).then_inc(in_landed[t], 16)
            grp = g_grp
            loads = [(parnat[C_NORM:C_NORM + 3 * L * KD, :], g_norm.rearrange("l i (k p) -> (l i k) p", p=P)),
                     (parnat[C_NORM + 3 * L * KD:C_GRP, :], g_final.rearrange("(k p) -> k p", p=P)),
                     (parnat[C_BDW:C_GLN, :], b_dw31.rearrange("l (c p) -> (l c) p", p=P)),
                     (parnat[C_GLN:C_BLN, :], g_ln.rearrange("l (c p) -> (l c) p", p=P)),
                     (parnat[C_BLN:C_SC3, :], b_ln.rearrange("l (c p) -> (l c) p", p=P)),
                     (parnat[C_SC3:N_PAR, :], w_sc3.rearrange("l t (c p) -> (l t c) p", p=P)),
                     (dwnat[0:N_DW, :], w_dw31.rearrange("l t (c p) -> (l t c) p", p=P)),
                     (sinknat[:, :], sinks.rearrange("(o l) h -> o (l h)", o=1).to_broadcast([P, L * HEADS]))]
            for l in range(L):
                c = C_GRP + l * KD
                for h in range(2):
                    loads.append((parnat[c:c + 4, 64 * h:64 * h + 64],
                                  grp[l, 256 * h:256 * h + 256].rearrange("(j q) -> j q", q=64)))
                loads.append((parnat[c + 4:c + KD, :], grp[l, D_ATTN:D].rearrange("(k p) -> k p", p=P)))
            for dst, src in loads:
                act.dma_start(dst, src).then_inc(par_landed, 16)
            assert len(loads) == PAR_LOADS

            def split(l, n, tiles):
                n, s, landed = n
                act.wait_ge(raw_landed[s % 2], landed)
                act.wait_ge(unit_done, l * UNITS + n + 1)
                nc.scalar.copy(wh[:, s % RING, 0:tiles, :], raw[:, s % RAW, 0:tiles, :]).then_inc(hi_ready, 1)

            def unit(l, n):
                return n, n, l * PER_SLOT[n % 2] + 16 * (n // 2 + 1) + extra(n)

            def loop_unit(l, n0, i, k):
                return n0 + 4 * i + k, k, l * PER_SLOT[k % 2] + 16 * (n0 // 2 + k // 2 + 1) + extra(n0 + k) + 32 * i

            def scaled_x(count, d, column):
                cnt, first = count
                act.wait_ge(x_ready, cnt + 1)
                nc.scalar.activation(xh[:, d, :], x[:, d, :], ACT.Copy, scale=column).then_inc(xh_ready, 1)
                squares(first, x[:, d, :])

            def squares(s, src, shaped=lambda ap: ap):
                n, parity, skip = s
                if not skip:
                    act.wait_ge(acc_ready, n - 1)
                    apart(act)
                nc.scalar.activation(shaped(sq[:, parity, :]), src, ACT.Square).then_inc(sq_ready, 1)

            def root(n, width=T):
                act.wait_ge(var_ready, n + 1)
                nc.scalar.activation(rstd[:, 0:width], rstd[:, 0:width], ACT.Sqrt).then_inc(root_ready, 1)

            def chunked(ap, t):
                return ap.rearrange("p (n q) -> p n q", q=CHUNK) if UQ <= t < UQ + 4 else ap

            def tile(t):
                return uq[:, :, t - UQ, :] if UQ <= t < UQ + 4 else u[:, t, :]

            act.wait_ge(par_t, 2)
            nc.scalar.copy(par[:, :], bank[STAT][:, 0:N_PAR])
            nc.scalar.copy(dw[:, :], bank[STAT][:, P:P + N_DW]).then_inc(const_ready, 1)
            act.wait_ge(const_ready, 3)
            for d in range(KD):
                scaled_x((d, (d, d % 2, d < 2)), d, par[:, C_NORM + d:C_NORM + d + 1])

            def ffn(l, j, last_tiles, last_ahead):
                base = FFN[j]

                def hidden(f, a, b):
                    F = (2 * l + j) * FT + f
                    act.wait_ge(gate_ready, F + 1)
                    nc.scalar.activation(gate[:, :], gate[:, :], ACT.Silu).then_inc(silu_ready, 1)
                    for n, tiles in (a, b):
                        split(l, n, tiles)
                    act.wait_ge(prod_ready, F + 1)
                    apart(act)
                    at_f = acth[:, f, :] if isinstance(f, int) else acth[:, bass.ds(f, 1), :].rearrange("p a t -> p (a t)")
                    nc.scalar.copy(at_f, prod[:, :]).then_inc(acth_ready, 1)

                root(l * NORMS + (NORM_FFN0, NORM_FFN1)[j])
                for f in range(2):
                    hidden(f, *[(unit(l, base + 4 + 2 * f + k), KD) for k in range(2)])
                with nc.scalar.Fori(1, FT // 2 - 1) as i:
                    for h in range(2):
                        hidden(2 * i + h, *[(loop_unit(l, base + 4, i, 2 * h + k), KD) for k in range(2)])
                for h in range(2):
                    f = FT - 2 + h
                    hidden(f, *[(unit(l, base + DOWN + 2 * h + k), HALF) for k in range(2)])

                def residual(d, after):
                    r = KD + l * RESES + RES[2 * j] + d
                    s = r
                    c = C_NORM + l * 3 * KD + (2 * j + 1) * KD + d
                    act.wait_ge(x_ready, r + 1)
                    apart(act)
                    xd = x[:, bass.ds(d, 1), :].rearrange("p a t -> p (a t)")
                    xhd = xh[:, bass.ds(d, 1), :].rearrange("p a t -> p (a t)")
                    nc.scalar.activation(xhd, xd, ACT.Copy, scale=par[:, bass.ds(c, 1)]).then_inc(xh_ready, 1)
                    return s, xd

                with nc.scalar.Fori(0, KD // 2 - 1) as i:
                    for h in range(2):
                        s, xd = residual(2 * i + h, None)
                        squares((s, h, False), xd)
                        for k in range(2):
                            split(l, loop_unit(l, base + DOWN + 4, i, 2 * h + k), HALF)
                for h in range(2):
                    s, xd = residual(KD - 2 + h, None)
                    squares((s, h, False), xd)
                    for n in last_ahead[h]:
                        split(l, unit(l, n), last_tiles)

            with nc.scalar.Fori(0, L) as l:
                for n in range(4):
                    split(l, unit(l, n), KD)
                ffn(l, 0, KD, [(W_IN, W_IN + 1), (W_IN + 2, W_IN + 3)])

                root(l * NORMS + NORM_MIX)
                for m in range(CT):
                    for k in range(2):
                        split(l, unit(l, W_IN + 4 + 2 * m + k), KD)
                    act.wait_ge(proj_read, l * PROJS + PROJ[1] + 2 * m + 2 + 4)
                    nc.scalar.activation(u[:, CG[m], :], u[:, CG[m], :], ACT.Sigmoid).then_inc(sig_ready, 1)
                for i in range(4, 10):
                    split(l, unit(l, W_IN + 4 + i), KD)

                def exps(p):
                    act.wait_ge(max_ready, l * PAIRS + p + 1)
                    if p:
                        act.wait_ge(probsT_ready, 2 * (l * PAIRS + p))
                    for kv in range(2):
                        for g in range(4):
                            keys = CHUNK if p == 0 and g < 2 else P
                            i = 4 * kv + g
                            nc.scalar.activation(probs[:, kv, g, 0:keys], bank[SCORES + kv][:, g * P:g * P + keys],
                                                 ACT.Exp, bias=soft[:, S_NEG, p, i:i + 1], scale=HEAD_DIM ** -0.5,
                                                 accum_out=soft[:, S_SUM, p, i:i + 1])
                    nc.scalar.activation(soft[:, S_ES, p, :], soft[:, S_SINK, p, :], ACT.Exp).then_inc(exp_ready, 1)

                def copy_probsT(p):
                    for kv in range(2):
                        act.wait_ge(probsT_ready, 2 * (l * PAIRS + p) + kv + 1)
                        if p:
                            act.wait_ge(o_ready, l * PAIRS + p)
                        nc.scalar.copy(probsT[:, kv, :, :].rearrange("p g q -> p (g q)"), bank[PROBS_T + kv][:, :])\
                            .then_inc(probsT_read, 1)

                def heads_squares(p):
                    act.wait_ge(o_read, l * PAIRS + p + 1)
                    if p:
                        act.wait_ge(sqa_sum, 3 * (l * PAIRS + p))
                    nc.scalar.activation(gate[:, :], uq[:, 2 * p:2 * p + 2, :, :].rearrange("p c j q -> p (c j q)"),
                                         ACT.Square).then_inc(sqa_ready, 1)

                def squares_b(norm, c, src):
                    if norm:
                        act.wait_ge(statb_ready, l * NORMS_B + norm)
                    elif c == 0:
                        act.wait_ge(acc_ready, KD + l * RESES + RES[1])
                    nc.scalar.activation(sq[:, c, :], src, ACT.Square).then_inc(sqb_ready, 1)

                def root_b(norm):
                    act.wait_ge(varb_ready, l * NORMS_B + norm + 1)
                    nc.scalar.activation(rstd_b[:, :], rstd_b[:, :], ACT.Sqrt).then_inc(rootb_ready, 1)

                def high_y(tiles, y0, ready0):
                    for i, t in enumerate(tiles):
                        act.wait_ge(y_ready, l * KD + ready0 + i + 1)
                        nc.scalar.copy(chunked(yh[:, y0 + i, :], t), tile(t)).then_inc(yh_ready, 1)

                for b in range(2):
                    act.wait_ge(v_t, 2 * l + b + 1)
                    nc.scalar.copy(vtok[:, 4 * b:4 * b + 4, :].rearrange("p n d -> p (n d)"), bank[PROBS_T + b][:, :])\
                        .then_inc(v_ready, 1)
                exps(0)
                split(l, unit(l, W_IN + 14), KD)
                split(l, unit(l, W_IN + 15), KD)
                copy_probsT(0)
                exps(1)
                split(l, unit(l, W_OUT + 0), KD)
                heads_squares(0)
                for c in range(CT):
                    act.wait_ge(ln_ready, l * 2 * CT + c + 1)
                    squares_b(NORM_LN, c, u[:, CA[c], :])
                split(l, unit(l, W_OUT + 1), KD)
                copy_probsT(1)
                exps(2)
                root_b(NORM_LN)
                for c in range(CT):
                    act.wait_ge(ln_ready, l * 2 * CT + CT + c + 1)
                    apart(act)
                    nc.scalar.activation(u[:, CA[c], :], u[:, CA[c], :], ACT.Silu,
                                         bias=par[:, bass.ds(l * CT + C_BLN + c, 1)],
                                         scale=par[:, bass.ds(l * CT + C_GLN + c, 1)]).then_inc(silu_conv, 1)
                for c in range(CT):
                    act.wait_ge(silu_conv, l * CT + c + 1)
                    squares_b(NORM_CONV, c, u[:, CA[c], :])
                split(l, unit(l, W_OUT + 2), KD)
                heads_squares(1)
                root_b(NORM_CONV)
                high_y(CA, 4, 0)
                split(l, unit(l, W_OUT + 3), KD)
                copy_probsT(2)
                exps(3)
                for c in range(CT):
                    act.wait_ge(sc_ready, l * CT + c + 1)
                    squares_b(NORM_SC, c, u[:, SB + c, :])
                heads_squares(2)
                root_b(NORM_SC)
                high_y([SB, SB + 1], 6, 2)
                copy_probsT(3)
                heads_squares(3)
                root(l * NORMS + NORM_ATTN)
                high_y([UQ + i for i in range(4)], 0, 4)

                for i, (g, d0, n) in enumerate(WO):
                    if g == ATTN_G:
                        for d in range(d0, d0 + n):
                            r = KD + l * RESES + RES[1] + d
                            act.wait_ge(x_ready, r + 1)
                            apart(act)
                            nc.scalar.activation(xh[:, d, :], x[:, d, :], ACT.Copy,
                                                 scale=par[:, bass.ds(l * 3 * KD + C_NORM + 2 * KD + d, 1)])\
                                .then_inc(xh_ready, 1)
                            if d < 2:
                                act.wait_ge(statb_ready, l * NORMS_B + NORMS_B)
                                nc.scalar.activation(sq[:, d % 2, :], x[:, d, :], ACT.Square).then_inc(sq_ready, 1)
                            else:
                                squares((r, d % 2, False), x[:, d, :])
                    split(l, unit(l, W_OUT + 4 + i), KD)
                ffn(l, 1, None, [(), ()])
            root(L * NORMS, NT)
            for t in range(NT):
                act.wait_ge(y_t, 2 * t + 1)
                if t == 0:
                    act.wait_ge(rstd_ready, L * NORMS + 1)
                nc.scalar.activation(ynat[:, t, 0:T], bank[2 * (t % 2)][:, :], ACT.Copy, scale=rstd[:, t:t + 1])\
                    .then_inc(y_read[0], 1)

        @block.vector
        def _(dve):
            dve.sem_inc(lo_ready, RAW)
            dve.sem_inc(proj_read, 4)

            def split(l, n, s, tiles):
                dve.wait_ge(hi_ready, l * UNITS + n + 1)
                nc.vector.tensor_tensor(wl[:, s % RING, 0:tiles, :], raw[:, s % RAW, 0:tiles, :],
                                        wh[:, s % RING, 0:tiles, :].bitcast(F32), ALU.subtract)\
                    .then_inc(lo_ready, 1)

            def low_x(cnt, d, column):
                xd, hd, ld = (t[:, d, :] if isinstance(d, int) else t[:, bass.ds(d, 1), :].rearrange("p a t -> p (a t)")
                              for t in (x, xh, xl))
                dve.wait_ge(xh_ready, cnt + 1)
                nc.vector.scalar_tensor_tensor(out=ld, in0=xd, scalar=column, in1=hd.bitcast(F32),
                                               op0=ALU.mult, op1=ALU.subtract).then_inc(xl_ready, 1)

            def variance(n, features, eps, width=T):
                dve.wait_ge(stat_ready, n + 1)
                nc.vector.tensor_scalar(rstd[:, 0:width], bank[STAT][:, 0:width], 1.0 / features, eps, ALU.mult,
                                        ALU.add).then_inc(var_ready, 1)

            def inverse(n, width=T):
                dve.wait_ge(root_ready, n + 1)
                nc.vector.reciprocal(rstd[:, 0:width], rstd[:, 0:width]).then_inc(rstd_ready, 1)
                dve.wait_ge(rstd_ready, n + 1)

            def rsqrt(n, features, eps):
                variance(n, features, eps)
                inverse(n)

            for d in range(KD):
                dve.wait_ge(in_t, d + 1)
                nc.vector.tensor_copy(x[:, d, :], bank[RES_BANK + d % 2][:, :]).then_inc(x_ready, 1)
            for d in range(KD):
                low_x(d, d, par[:, C_NORM + d:C_NORM + d + 1])
            dve.wait_ge(par_landed, 16 * PAR_LOADS)
            for h in range(2):
                src = sinknat[64 * h:64 * h + 64, :].rearrange("p (c r s) -> p c r s", r=2, s=2)[:, :, :, h]
                to = sink[64 * h:64 * h + 64, :].rearrange("p (c n r) -> p c n r", n=2, r=2)
                for n in range(2):
                    nc.vector.tensor_copy(to[:, :, n, :], src).then_inc(sinks_ready, 1)

            def ffn(l, j, last_tiles, last_ahead):
                base = FFN[j]

                def hidden(f, ahead):
                    F = (2 * l + j) * FT + f
                    q = l * PROJS + PROJ[2 * j] + 2 * f
                    n = l * UNITS + base + 2 * f + RING
                    b = 2 * (f % 2) if isinstance(f, int) else 2 * ahead[1]
                    dve.wait_ge(unit_done, n + 1)
                    nc.vector.tensor_tensor(gate[:, :], bank[b][:, :], rstd[:, :], ALU.mult).then_inc(gate_ready, 1)
                    dve.wait_ge(unit_done, n + 2)
                    if not (isinstance(f, int) and f == 0):
                        dve.wait_ge(actl_ready, F)
                    nc.vector.tensor_tensor(prod[:, :], bank[b + 1][:, :], rstd[:, :], ALU.mult).then_inc(proj_read, 2)
                    for a, s, tiles in ahead[0]:
                        split(l, a, s, tiles)
                    dve.wait_ge(silu_ready, F + 1)
                    dve.wait_ge(proj_read, q + 6)
                    nc.vector.tensor_tensor(prod[:, :], gate[:, :], prod[:, :], ALU.mult).then_inc(prod_ready, 1)
                    dve.wait_ge(acth_ready, F + 1)
                    hi, lo = (t[:, f, :] if isinstance(f, int) else t[:, bass.ds(f, 1), :].rearrange("p a t -> p (a t)")
                              for t in (acth, actl))
                    nc.vector.tensor_tensor(lo, prod[:, :], hi.bitcast(F32), ALU.subtract).then_inc(actl_ready, 1)

                rsqrt(l * NORMS + (NORM_FFN0, NORM_FFN1)[j], D, RMS_EPS)
                for f in range(2):
                    hidden(f, ([(base + 4 + 2 * f + k, 2 * f + k, KD) for k in range(2)], f))
                with nc.vector.Fori(1, FT // 2 - 1) as i:
                    for h in range(2):
                        hidden(2 * i + h, ([(4 * i + base + 4 + 2 * h + k, 2 * h + k, KD) for k in range(2)], h))
                for h in range(2):
                    hidden(FT - 2 + h, ([(base + DOWN + 2 * h + k, 2 * h + k, HALF) for k in range(2)], h))

                def residual(d, h):
                    r = l * RESES + RES[2 * j] + d
                    dve.wait_ge(unit_done, l * UNITS + base + DOWN + 2 * d + RING + 2)
                    xd = x[:, bass.ds(d, 1), :].rearrange("p a t -> p (a t)")
                    nc.vector.scalar_tensor_tensor(out=xd, in0=bank[RES_BANK + h][:, :], scalar=0.5, in1=xd,
                                                   op0=ALU.mult, op1=ALU.add).then_inc(x_ready, 1)
                    low_x(KD + r, d, par[:, bass.ds(l * 3 * KD + C_NORM + (2 * j + 1) * KD + d, 1)])

                with nc.vector.Fori(0, KD // 2 - 1) as i:
                    for h in range(2):
                        residual(2 * i + h, h)
                        for k in range(2):
                            split(l, 4 * i + base + DOWN + 4 + 2 * h + k, 2 * h + k, HALF)
                for h in range(2):
                    residual(KD - 2 + h, h)
                    for n in last_ahead[h]:
                        split(l, n, n, last_tiles)

            CONV_STEPS = CT + CT * TAPS

            with nc.vector.Fori(0, L) as l:
                for n in range(4):
                    split(l, n, n, KD)
                ffn(l, 0, KD, [(W_IN, W_IN + 1), (W_IN + 2, W_IN + 3)])

                rsqrt(l * NORMS + NORM_MIX, D, RMS_EPS)
                own = [0]

                def step(inst):
                    own[0] += 1
                    inst.then_inc(vec_step, 1)

                def steps_done(back=0):
                    dve.wait_ge(vec_step, l * VEC_STEPS + own[0] - back)

                def take(i):
                    dve.wait_ge(unit_done, l * UNITS + W_IN + i + 1 + RING)
                    b = i % 4 if i < SB else i % 2
                    if UQ <= i < UQ + 4:
                        nc.vector.tensor_tensor(uq[:, :, i - UQ, :], chunked(bank[b][:, :], i), chunked(rstd[:, :], i),
                                                ALU.mult).then_inc(proj_read, 1)
                    else:
                        nc.vector.tensor_tensor(u[:, i, :], bank[b][:, :], rstd[:, :], ALU.mult).then_inc(proj_read, 1)

                def taken(i):
                    dve.wait_ge(proj_read, l * PROJS + PROJ[1] + i + 1 + 4)

                def chunked(ap, t):
                    return ap.rearrange("p (n q) -> p n q", q=CHUNK) if UQ <= t < UQ + 4 else ap

                def tile(t):
                    return uq[:, :, t - UQ, :] if UQ <= t < UQ + 4 else u[:, t, :]

                def taps(block):
                    before = 1 + sum(TAP_BLOCKS[:block])
                    with nc.vector.Fori(0, TAP_BLOCKS[block]) as t:
                        for c in range(CT):
                            dve.wait_ge(conv_step, l * CONV_STEPS + CT * t + CT * before + c + 1)
                            nc.vector.scalar_tensor_tensor(
                                out=u[:, CA[c], :], in0=z[:, c, bass.ds(t + before, T)],
                                scalar=dw[:, bass.ds(l * TAPS * CT + CT * t + CT * before + c, 1)],
                                in1=u[:, CA[c], :], op0=ALU.mult, op1=ALU.add).then_inc(conv_step, 1)

                def maxima(p):
                    dve.wait_ge(scores_ready, l * PAIRS + p + 1)
                    for kv in range(2):
                        sc = bank[SCORES + kv][:, :].rearrange("p (g k) -> p g k", k=P)
                        if p == 0:
                            nc.vector.reduce_max(soft[:, S_MAX, p, 4 * kv:4 * kv + 2], sc[:, 0:2, 0:CHUNK], axis=AX.X)
                            r = nc.vector.reduce_max(soft[:, S_MAX, p, 4 * kv + 2:4 * kv + 4], sc[:, 2:4, :], axis=AX.X)
                        else:
                            r = nc.vector.reduce_max(soft[:, S_MAX, p, 4 * kv:4 * kv + 4], sc, axis=AX.X)
                    step(r)
                    sk = sink[:, bass.ds(l * KV_HEADS * 4, KV_HEADS * 4)]
                    steps_done()
                    step(nc.vector.scalar_tensor_tensor(out=soft[:, S_M, p, :], in0=soft[:, S_MAX, p, :],
                                                        scalar=HEAD_DIM ** -0.5, in1=sk, op0=ALU.mult, op1=ALU.max))
                    steps_done()
                    nc.vector.tensor_scalar(soft[:, S_NEG, p, :], soft[:, S_M, p, :], -1.0, None, ALU.mult)
                    nc.vector.tensor_tensor(soft[:, S_SINK, p, :], sk, soft[:, S_M, p, :], ALU.subtract)\
                        .then_inc(max_ready, 1)

                def normalise(p):
                    dve.wait_ge(exp_ready, l * PAIRS + p + 1)
                    step(nc.vector.tensor_tensor(soft[:, S_DEN, p, :], soft[:, S_SUM, p, :], soft[:, S_ES, p, :],
                                                 ALU.add))
                    steps_done()
                    step(nc.vector.reciprocal(soft[:, S_R, p, :], soft[:, S_DEN, p, :]))
                    steps_done()
                    for i in range(8):
                        t = nc.vector.tensor_scalar(probs[:, i // 4, i % 4, :], probs[:, i // 4, i % 4, :],
                                                    soft[:, S_R, p, i:i + 1], None, ALU.mult)
                    t.then_inc(probs_ready, 1)

                def read_heads(p):
                    dve.wait_ge(o_ready, l * PAIRS + p + 1)
                    nc.vector.tensor_copy(uq[:, 2 * p:2 * p + 2, :, :].rearrange("p c j q -> p (c j q)"),
                                          bank[HEADS_OUT][:, :]).then_inc(o_read, 1)

                def variance_b(norm, eps):
                    dve.wait_ge(statb_ready, l * NORMS_B + norm + 1)
                    nc.vector.tensor_scalar(rstd_b[:, :], bank[STAT][:, :], 1.0 / D_CONV, eps, ALU.mult, ALU.add)\
                        .then_inc(varb_ready, 1)

                def inverse_b(norm):
                    dve.wait_ge(rootb_ready, l * NORMS_B + norm + 1)
                    nc.vector.reciprocal(rstd_b[:, :], rstd_b[:, :]).then_inc(rstdb_ready, 1)
                    dve.wait_ge(rstdb_ready, l * NORMS_B + norm + 1)

                def scale_y(tiles, y0, r):
                    for i, t in enumerate(tiles):
                        nc.vector.scalar_tensor_tensor(out=tile(t), in0=tile(t),
                                                       scalar=par[:, bass.ds(l * KD + C_GRP + y0 + i, 1)],
                                                       in1=chunked(r[:, :], t), op0=ALU.mult, op1=ALU.mult)\
                            .then_inc(y_ready, 1)

                def low_y(tiles, y0, ready0):
                    for i, t in enumerate(tiles):
                        dve.wait_ge(yh_ready, l * KD + ready0 + i + 1)
                        nc.vector.tensor_tensor(chunked(yl[:, y0 + i, :], t), tile(t),
                                                chunked(yh[:, y0 + i, :].bitcast(F32), t), ALU.subtract)\
                            .then_inc(yl_ready, 1)

                def short_conv(c):
                    step(nc.vector.tensor_tensor(cx[:, c, SC_TAPS - 1:SC_TAPS - 1 + T], u[:, SC + c, :],
                                                 u[:, SX + c, :], ALU.mult))
                    for t in range(SC_TAPS):
                        steps_done()
                        w = par[:, bass.ds(l * SC_TAPS * CT + C_SC3 + CT * t + c, 1)]
                        if t == 0:
                            step(nc.vector.tensor_scalar(u[:, SC + c, :], cx[:, c, 0:T], w, None, ALU.mult))
                        else:
                            step(nc.vector.scalar_tensor_tensor(out=u[:, SC + c, :], in0=cx[:, c, t:t + T], scalar=w,
                                                                in1=u[:, SC + c, :], op0=ALU.mult, op1=ALU.add))
                    steps_done()
                    nc.vector.tensor_tensor(u[:, SB + c, :], u[:, SB + c, :], u[:, SC + c, :], ALU.mult)\
                        .then_inc(sc_ready, 1)

                for m in range(CT):
                    for k in range(2):
                        take(2 * m + k)
                    for k in range(2):
                        split(l, W_IN + 4 + 2 * m + k, 2 * m + k, KD)
                    dve.wait_ge(sig_ready, l * CT + m + 1)
                    if m == 0:
                        dve.wait_ge(pads_zero, l + 1)
                    nc.vector.tensor_tensor(z[:, m, TAPS - 1:TAPS - 1 + T], u[:, CA[m], :], u[:, CG[m], :], ALU.mult)\
                        .then_inc(conv_step, 1)
                for c in range(CT):
                    dve.wait_ge(conv_step, l * CONV_STEPS + c + 1)
                    nc.vector.tensor_scalar(u[:, CA[c], :], z[:, c, 0:T], dw[:, bass.ds(l * TAPS * CT + c, 1)],
                                            par[:, bass.ds(l * CT + C_BDW + c, 1)], ALU.mult, ALU.add)\
                        .then_inc(conv_step, 1)
                for i in range(4, 10):
                    take(i)
                    split(l, W_IN + 4 + i, i % 4, KD)
                    if i % 2:
                        taps(i // 2 - 2)
                maxima(0)
                take(10)
                split(l, W_IN + 14, 2, KD)
                taps(3)
                normalise(0)
                take(11)
                split(l, W_IN + 15, 3, KD)
                taps(4)
                maxima(1)
                take(12)
                split(l, W_OUT + 0, 0, KD)
                taps(5)
                normalise(1)
                read_heads(0)
                dve.wait_ge(mean_ready, l + 1)
                for c in range(CT):
                    nc.vector.scalar_tensor_tensor(out=u[:, CA[c], :], in0=bank[STAT][:, :], scalar=-1.0 / D_CONV,
                                                   in1=u[:, CA[c], :], op0=ALU.mult, op1=ALU.add).then_inc(ln_ready, 1)
                take(13)
                split(l, W_OUT + 1, 1, KD)
                maxima(2)
                variance_b(NORM_LN, LN_EPS)
                inverse_b(NORM_LN)
                dve.wait_ge(ln_ready, l * 2 * CT + CT)
                for c in range(CT):
                    nc.vector.tensor_tensor(u[:, CA[c], :], u[:, CA[c], :], rstd_b[:, :], ALU.mult).then_inc(ln_ready, 1)
                take(14)
                split(l, W_OUT + 2, 2, KD)
                read_heads(1)
                normalise(2)
                taken(14)
                short_conv(0)
                variance_b(NORM_CONV, RMS_EPS)
                inverse_b(NORM_CONV)
                scale_y(CA, 4, rstd_b)
                low_y(CA, 4, 0)
                take(15)
                split(l, W_OUT + 3, 3, KD)
                maxima(3)
                taken(15)
                short_conv(1)
                read_heads(2)
                normalise(3)
                variance_b(NORM_SC, RMS_EPS)
                inverse_b(NORM_SC)
                scale_y([SB, SB + 1], 6, rstd_b)
                low_y([SB, SB + 1], 6, 2)
                read_heads(3)
                rsqrt(l * NORMS + NORM_ATTN, D_ATTN, RMS_EPS)
                scale_y([UQ + i for i in range(4)], 0, rstd)
                low_y([UQ + i for i in range(4)], 0, 4)
                assert own[0] == VEC_STEPS

                for i, (g, d0, n) in enumerate(WO):
                    if g == ATTN_G:
                        dve.wait_ge(unit_done, l * UNITS + W_OUT + i + 1 + RING)
                        for d in range(d0, d0 + n):
                            nc.vector.tensor_tensor(x[:, d, :], bank[d][:, :], x[:, d, :], ALU.add).then_inc(x_ready, 1)
                        for d in range(d0, d0 + n):
                            low_x(KD + l * RESES + RES[1] + d, d,
                                  par[:, bass.ds(l * 3 * KD + C_NORM + 2 * KD + d, 1)])
                    split(l, W_OUT + 4 + i, i % 4, KD)
                ffn(l, 1, None, [(), ()])

            for d in range(KD):
                c = C_NORM + 3 * L * KD + d
                nc.vector.tensor_scalar(yT[:, d, :], x[:, d, :], par[:, c:c + 1], None, ALU.mult).then_inc(y_scaled, 1)
            variance(L * NORMS, D, RMS_EPS, NT)
            inverse(L * NORMS, NT)
            for t in range(NT):
                dve.wait_ge(y_t, 2 * t + 2)
                nc.vector.tensor_scalar(ynat[:, t, T:2 * T], bank[2 * (t % 2) + 1][:, :], rstd[:, t:t + 1], None,
                                        ALU.mult).then_inc(y_read[1], 1)

        @block.tensor
        def _(pe):
            pe.sem_inc(unit_done, RING)

            pe.wait_ge(const_ready, 2)
            pe.wait_ge(par_landed, 16 * PAR_LOADS)
            nc.tensor.transpose(bank[STAT][:, 0:N_PAR], parnat[0:N_PAR, :], ident[0:N_PAR, 0:N_PAR]).then_inc(par_t, 1)
            nc.tensor.transpose(bank[STAT][:, P:P + N_DW], dwnat[0:N_DW, :], ident[0:N_DW, 0:N_DW]).then_inc(par_t, 1)
            for d in range(KD):
                if d >= 2:
                    pe.wait_ge(x_ready, d - 1)
                for t in range(NT):
                    if d == 0:
                        pe.wait_ge(in_landed[t], 16)
                    mm = nc.tensor.transpose(bank[RES_BANK + d % 2][:, t * P:(t + 1) * P],
                                             xnat[:, t, d * P:(d + 1) * P], ident[:, :])
                mm.then_inc(in_t, 1)

            def tile_product(o, s, k, ah, al, first, last):
                nc.tensor.matmul(o, wh[:, s, k, :], ah, start=first, stop=False)
                nc.tensor.matmul(o, wh[:, s, k, :], al, start=False, stop=False)
                return nc.tensor.matmul(o, wl[:, s, k, :], ah, start=False, stop=last)

            def projection(l, n, s, b, reads, done):
                pe.wait_ge(lo_ready, l * UNITS + n + 1 + RAW)
                pe.wait_ge(proj_read, reads)
                for k in range(KD):
                    pe.wait_ge(xl_ready, done + k + 1)
                    mm = tile_product(bank[b][:, :], s, k, xh[:, k, :], xl[:, k, :], k == 0, k == KD - 1)
                mm.then_inc(unit_done, 1)

            def stat(n, squares_done):
                pe.wait_ge(acc_ready, squares_done)
                nc.tensor.matmul(bank[STAT][:, :], ones[:, :], acc[:, :], start=True, stop=True)\
                    .then_inc(stat_ready, 1)

            def pair(l, n, q, h, done):
                for k in range(2):
                    projection(l, n + k, 2 * h + k, 2 * h + k, l * PROJS + q + k + 1, done)

            def ffn(l, j):
                base, q0 = FFN[j], PROJ[2 * j]
                done = l * RESES + (0, 2 * KD)[j]
                pair(l, base, q0, 0, done)
                stat(l * NORMS + (NORM_FFN0, NORM_FFN1)[j], done + KD)
                pair(l, base + 2, q0 + 2, 1, done)
                with nc.tensor.Fori(1, FT // 2) as i:
                    for h in range(2):
                        pair(l, 4 * i + base + 2 * h, 4 * i + q0 + 2 * h, h, done)
                with nc.tensor.Fori(0, KD // 2) as i:
                    for h in range(2):
                        d = 2 * i + h
                        r = l * RESES + RES[2 * j] + d
                        pe.wait_ge(x_ready, r + KD - 1)
                        for k in range(2):
                            s = 2 * h + k
                            pe.wait_ge(lo_ready, l * UNITS + 2 * d + base + DOWN + k + 1 + RAW)
                            for t in range(HALF):
                                f = k * HALF + t
                                pe.wait_ge(actl_ready, (2 * l + j) * FT + f + 1)
                                mm = tile_product(bank[RES_BANK + h][:, :], s, t, acth[:, f, :], actl[:, f, :],
                                                  f == 0, f == FT - 1)
                            mm.then_inc(unit_done, 1)

            with nc.tensor.Fori(0, L) as l:
                ffn(l, 0)
                done = l * RESES + KD
                def take_in(i):
                    projection(l, W_IN + i, i % 4, i % 4 if i < SB else i % 2,
                               l * PROJS + PROJ[1] + i + 1 + (0 if i < SB else 2), done)

                def stat_b(norm):
                    for c in range(CT):
                        pe.wait_ge(sqb_ready, l * NORMS_B * CT + norm * CT + c + 1)
                        mm = nc.tensor.matmul(bank[STAT][:, :], ones[:, :], sq[:, c, :], start=c == 0, stop=c == CT - 1)
                    mm.then_inc(statb_ready, 1)

                def scores(p):
                    if p:
                        pe.wait_ge(exp_ready, l * PAIRS + p)
                    for kv in range(2):
                        rows = slice(64 * kv, 64 * kv + 64)
                        for c in range(2):
                            n = 2 * p + c
                            k0 = max(0, (n - 1) * CHUNK)
                            keys = (n + 1) * CHUNK - k0
                            for pr in range(2):
                                g = (2 * c + pr) * P
                                mm = nc.tensor.matmul(
                                    bank[SCORES + kv][:, g:g + keys],
                                    uq[rows, n, 2 * pr:2 * pr + 2, :].rearrange("p j q -> p (j q)"),
                                    u[rows, UK, k0:k0 + keys], start=True, stop=True)
                    mm.then_inc(scores_ready, 1)

                def transpose_probs(p):
                    pe.wait_ge(probs_ready, l * PAIRS + p + 1)
                    if p:
                        pe.wait_ge(probsT_read, 2 * (l * PAIRS + p))
                    else:
                        pe.wait_ge(v_ready, 2 * l + 2)
                    for kv in range(2):
                        for g in range(4):
                            mm = nc.tensor.transpose(bank[PROBS_T + kv][:, g * P:(g + 1) * P], probs[:, kv, g, :],
                                                     ident[:, :])
                        mm.then_inc(probsT_ready, 1)

                def heads(p):
                    if p:
                        pe.wait_ge(o_read, l * PAIRS + p)
                    for kv in range(2):
                        pe.wait_ge(probsT_read, 2 * (l * PAIRS + p) + kv + 1)
                        apart(pe)
                        for c in range(2):
                            n = 2 * p + c
                            K = CHUNK if n == 0 else P
                            mm = nc.tensor.matmul(bank[HEADS_OUT][64 * kv:64 * kv + 64, c * 256:(c + 1) * 256],
                                                  vtok[0:K, n, 64 * kv:64 * kv + 64],
                                                  probsT[0:K, kv, 2 * c:2 * c + 2, :], start=True, stop=True)
                    mm.then_inc(o_ready, 1)

                def project_y(i):
                    g, d0, n = WO[i]
                    tiles = GROUP_TILES[g]
                    pe.wait_ge(lo_ready, l * UNITS + W_OUT + i + 1 + RAW)
                    for dd in range(n):
                        for k, y in enumerate(tiles):
                            pe.wait_ge(yl_ready, l * KD + (0, 2, 4)[g] + k + 1)
                            mm = tile_product(bank[d0 + dd][:, :], i % RING, k * n + dd, yh[:, y, :], yl[:, y, :],
                                              g == CONV_G and k == 0, g == ATTN_G and k == 3)
                    mm.then_inc(unit_done, 1)

                take_in(0)
                take_in(1)
                stat(l * NORMS + NORM_MIX, done + KD)
                for i in range(2, 10):
                    take_in(i)
                pe.wait_ge(proj_read, l * PROJS + PROJ[1] + 10 + 4)
                for b in range(2):
                    for i in range(4):
                        t0 = max(0, (4 * b + i - 1) * CHUNK)
                        mm = nc.tensor.transpose(bank[PROBS_T + b][:, i * P:(i + 1) * P], u[:, UV, t0:t0 + P],
                                                 ident[:, :])
                    mm.then_inc(v_t, 1)
                scores(0)
                take_in(10)
                take_in(11)
                transpose_probs(0)
                scores(1)
                take_in(12)
                heads(0)
                pe.wait_ge(conv_step, l * CONV_STEPS_ALL + CONV_STEPS_ALL)
                for c in range(CT):
                    mm = nc.tensor.matmul(bank[STAT][:, :], ones[:, :], u[:, CA[c], :], start=c == 0, stop=c == CT - 1)
                mm.then_inc(mean_ready, 1)
                take_in(13)
                transpose_probs(1)
                scores(2)
                pe.wait_ge(ln_ready, l * 2 * CT + CT)
                stat_b(NORM_LN)
                take_in(14)
                heads(1)
                stat_b(NORM_CONV)
                take_in(15)
                transpose_probs(2)
                scores(3)
                heads(2)
                stat_b(NORM_SC)
                pe.wait_ge(proj_read, l * PROJS + PROJ[2] + 4)
                pe.wait_ge(exp_ready, (l + 1) * PAIRS)
                project_y(0)
                transpose_probs(3)
                heads(3)
                project_y(1)
                pe.wait_ge(sqa_sum, (l + 1) * 3 * PAIRS)
                nc.tensor.matmul(bank[STAT][:, :], ones[:, :], prod[:, :], start=True, stop=True)\
                    .then_inc(stat_ready, 1)
                for i in range(2, KD):
                    project_y(i)
                ffn(l, 1)

            def tokens(t):
                for h in range(2):
                    if t >= 2:
                        pe.wait_ge(y_read[h], t - 1)
                    for k in range(4):
                        pe.wait_ge(y_scaled, 4 * h + k + 1)
                        mm = nc.tensor.transpose(bank[2 * (t % 2) + h][:, k * P:(k + 1) * P],
                                                 yT[:, 4 * h + k, t * P:(t + 1) * P], ident[:, :])
                    mm.then_inc(y_t, 1)

            tokens(0)
            pe.wait_ge(acc_ready, L * RESES + KD)
            for t in range(NT):
                mm = nc.tensor.matmul(bank[STAT][:, t:t + 1], acc[:, t * P:(t + 1) * P], ones[:, 0:1],
                                      start=True, stop=True)
            mm.then_inc(stat_ready, 1)
            for t in range(1, NT):
                tokens(t)


PAR_LOADS = 14
CONV_STEPS_ALL = 2 + 2 * 31
VEC_STEPS = 4 * 4 + 2 * 4


_INS = ["x", "g_norm", "w_ff_gate", "w_ff_up", "w_ff_down", "w_in", "w_dw31", "b_dw31",
        "g_ln_conv", "b_ln_conv", "w_sc3", "sinks", "g_grp", "w_out", "g_final"]


def kernel(**inputs):
    import numpy as _np
    import concourse.bacc as _bacc
    from concourse import mybir as _mybir
    from concourse.bass_utils import run_bass_kernel_spmd as _run

    nc = _bacc.Bacc("TRN2", target_bir_lowering=False, num_devices=1)
    arrays, args = {}, []
    for name in _INS:
        a = _np.ascontiguousarray(inputs[name])
        arrays[f"in_{name}_dram"] = a
        args.append(nc.dram_tensor(f"in_{name}_dram", a.shape, _mybir.dt.from_np(a.dtype), kind="ExternalInput").ap())
    shape = inputs["x"].shape
    args.append(nc.dram_tensor("out_dram", shape, _mybir.dt.float32, kind="ExternalOutput").ap())
    encoder_trunk(nc, *args)
    r = _run(nc, [arrays], core_ids=[0])
    return r.results[0]["out_dram"]
```

```python
from contextlib import ExitStack

import concourse.bass as bass
from concourse import mybir

F32 = mybir.dt.float32
F32R = mybir.dt.float32r
ALU = mybir.AluOpType
ACT = mybir.ActivationFunctionType
AX = mybir.AxisListType

P = 128
RMS_EPS = 1e-6
LN_EPS = 1e-5
CHUNK = 64
HEADS, KV_HEADS, HEAD_DIM = 8, 2, 64

RAW = 2
RING = 4


def encoder_trunk(nc, x_in, g_norm, w_gate, w_up, w_down, w_in, w_dw31, b_dw31, g_ln, b_ln, w_sc3,
                  sinks, g_grp, w_out, g_final, out):
    _, T, D = x_in.shape
    L, _, _, FF = w_gate.shape
    N_IN = w_in.shape[2]
    KD = D // P
    FT = FF // P
    HALF = FT // 2
    NT = T // P
    UT = N_IN // P
    TAPS = w_dw31.shape[1]
    SC_TAPS = w_sc3.shape[1]
    D_ATTN = HEADS * HEAD_DIM
    D_CONV = w_dw31.shape[2]
    CT = D_CONV // P
    assert (KD, NT, UT, CT) == (8, 4, 16, 2) and T == 512 and FT % 2 == 0 and D_ATTN == 4 * P

    CA, CG, UK, UQ, UV = [0, 2], [1, 3], 4, 5, 9
    SC, SX, SB = [10, 13], [11, 14], [12, 15]
    TWO_BANKS = 10
    COL = D_ATTN + 2 * KV_HEADS * HEAD_DIM
    COLS = ([COL, COL + 2 * P, COL + P, COL + 3 * P, D_ATTN] + [None] * 4
            + [D_ATTN + P] + [COL + (4 + i) * P for i in (2, 4, 0, 3, 5, 1)])

    DOWN, W_IN, W_OUT = 2 * FT, 2 * FT + 2 * KD, 2 * FT + 2 * KD + UT
    FFN = [0, W_OUT + KD]
    UNITS = FFN[1] + 2 * FT + 2 * KD
    PROJ = [0, 2 * FT, 2 * FT + UT]
    PROJS = PROJ[2] + 2 * FT
    RES = [0, KD, 2 * KD]
    RESES = 3 * KD
    NORM_FFN0, NORM_MIX, NORM_ATTN, NORM_FFN1 = range(4)
    NORMS = 4
    RSTDS = 3
    NORM_SC, NORM_LN, NORM_CONV = range(3)
    NORMS_B = 3
    PAIRS = T // (2 * CHUNK)
    TAP_BLOCKS = [3, 2, 3, 2, 3, 1, 2, 2, 2, 2, 1, 2, 1, 1, 2, 1]
    assert sum(TAP_BLOCKS) == TAPS - 1

    C_NORM = 0
    GAINS = 3 * L * KD
    C_GRP = C_NORM + GAINS + KD
    C_BDW = C_GRP + L * KD
    C_GLN = C_BDW + L * CT
    C_BLN = C_GLN + L * CT
    C_SC3 = C_BLN + L * CT
    N_PAR = C_SC3 + L * SC_TAPS * CT
    N_DW = L * TAPS * CT
    assert N_PAR <= P and N_DW <= P and UNITS % RING == 0

    with ExitStack() as ctx:
        def sb(name, shape, dt=F32):
            return ctx.enter_context(nc.sbuf_tensor(name, shape, dt))

        def sem(name):
            return ctx.enter_context(nc.semaphore(name))

        x = sb("x", [P, KD, T])
        xh = sb("xh", [P, KD, T], F32R)
        xl = sb("xl", [P, KD, T], F32R)
        raw = sb("raw", [P, RAW, HALF, P])
        wh = sb("wh", [P, RING, HALF, P], F32R)
        wl = sb("wl", [P, RING, HALF, P], F32R)
        sq = sb("sq", [P, 2, T])
        acc = sb("acc", [P, T])
        rstd = sb("rstd", [P, T])
        gate = sb("gate", [P, T])
        prod = sb("prod", [P, T])
        small = sb("small", [P, 2, 2, NT])
        par = sb("par", [P, N_PAR])
        dw = sb("dw", [P, N_DW])
        ident = sb("ident", [P, P])
        ones = sb("ones", [P, P])
        diag_b = sb("diag_b", [P, T])
        sink = sb("sink", [P, L * KV_HEADS * 4])

        region = sb("region", [P, 2 * FT * T])
        offset = [0]

        def at(name, shape, dt=F32):
            size = 4
            for n in shape[1:]:
                size *= n
            t = nc.alloc_sbuf_tensor_at(name, shape, dt, offset=REGION + offset[0])
            offset[0] += size
            assert offset[0] <= 2 * FT * T * 4
            return t

        REGION = nc.sbuf_base - 2 * FT * T * 4
        acth = at("acth", [P, FT, T], F32R)
        actl = at("actl", [P, FT, T], F32R)
        offset[0] = 0
        u = at("u", [P, UT, T])
        uq = u[:, UQ:UQ + 4, :].rearrange("p j t -> p (j t)").rearrange("p (n j q) -> p n j q", j=4, q=CHUNK)
        yh = at("yh", [P, KD, T], F32R)
        yl = at("yl", [P, KD, T], F32R)
        z = at("z", [P, CT, TAPS - 1 + T + 2])
        cx = at("cx", [P, CT, SC_TAPS - 1 + T + 6])
        probs = at("probs", [P, 2, 4, P])
        probsT = at("probsT", [P, 2, 4, P])
        vtok = at("vtok", [P, 2 * PAIRS, P])
        soft = at("soft", [P, 8, PAIRS, 8])
        S_MAX, S_M, S_NEG, S_SINK, S_SUM, S_ES, S_DEN, S_R = range(8)
        offset[0] = 0
        xnat = at("xnat", [P, NT, D])
        parnat = at("parnat", [P, P])
        dwnat = at("dwnat", [P, P])
        sinknat = at("sinknat", [P, L * HEADS])
        offset[0] = 0
        ynat = at("ynat", [P, NT, D])

        bank = [ctx.enter_context(nc.psum_tensor(f"bank{i}", [P, T], F32)) for i in range(8)]
        X_BANKS = [4, 5, 2, 3, 1, 4, 5, 2]
        RES_BANK, STAT, SCORES, PROBS_T, HEADS_OUT = 4, 6, 2, 4, 7

        raw_landed = [sem(f"raw_landed{i}") for i in range(RAW)]
        in_landed = [sem(f"in_landed{i}") for i in range(NT)]
        gains_landed = sem("gains_landed")
        par_landed = sem("par_landed")
        out_landed = sem("out_landed")
        hi_ready = sem("hi_ready")
        lo_ready = sem("lo_ready")
        unit_done = sem("unit_done")
        proj_read = sem("proj_read")
        x_ready = sem("x_ready")
        xh_ready = sem("xh_ready")
        xl_ready = sem("xl_ready")
        sq_ready = sem("sq_ready")
        acc_ready = sem("acc_ready")
        stat_ready = sem("stat_ready")
        root_ready = sem("root_ready")
        inv_ready = sem("inv_ready")
        diag_ready = sem("diag_ready")
        spread_ready = sem("spread_ready")
        rstd_ready = sem("rstd_ready")
        gate_ready = sem("gate_ready")
        silu_ready = sem("silu_ready")
        prod_ready = sem("prod_ready")
        acth_ready = sem("acth_ready")
        actl_ready = sem("actl_ready")
        const_ready = sem("const_ready")
        ident_zero = sem("ident_zero")
        par_t = sem("par_t")
        par_ready = sem("par_ready")
        in_t = sem("in_t")
        sinks_ready = sem("sinks_ready")
        sig_ready = sem("sig_ready")
        pads_zero = sem("pads_zero")
        gated = sem("gated")
        first_tap = sem("first_tap")
        conv_step = sem("conv_step")
        vec_step = sem("vec_step")
        mean_ready = sem("mean_ready")
        ln_ready = sem("ln_ready")
        silu_conv = sem("silu_conv")
        sc_ready = sem("sc_ready")
        sqb_ready = sem("sqb_ready")
        statb_ready = sem("statb_ready")
        rootb_ready = sem("rootb_ready")
        invb_ready = sem("invb_ready")
        diagb_ready = sem("diagb_ready")
        spreadb_ready = sem("spreadb_ready")
        NORM_A = (stat_ready, root_ready, inv_ready, diag_ready, spread_ready, rstd, 0, STAT)
        NORM_B = (statb_ready, rootb_ready, invb_ready, diagb_ready, spreadb_ready, diag_b, 1, STAT)
        NORM_O = (stat_ready, root_ready, inv_ready, diag_ready, spread_ready, rstd, 0, HEADS_OUT)
        y_ready = sem("y_ready")
        yh_ready = sem("yh_ready")
        yl_ready = sem("yl_ready")
        v_t = sem("v_t")
        v_ready = sem("v_ready")
        scores_ready = sem("scores_ready")
        max_ready = sem("max_ready")
        exp_ready = sem("exp_ready")
        den_ready = sem("den_ready")
        probs_ready = sem("probs_ready")
        probsT_ready = sem("probsT_ready")
        probsT_read = sem("probsT_read")
        o_ready = sem("o_ready")
        o_read = sem("o_read")
        sqa_ready = sem("sqa_ready")
        sqa_sum = sem("sqa_sum")
        passed = sem("passed")
        y_scaled = sem("y_scaled")
        y_t = [sem("y_t0"), sem("y_t1")]
        y_read = [sem("y_read_scalar"), sem("y_read_vector")]

        block = ctx.enter_context(nc.Block())

        def apart(eng):
            eng.sem_inc(passed, 1)

        gate_v = w_gate.rearrange("l j (k p) f -> l j p k f", p=P)
        up_v = w_up.rearrange("l j (k p) f -> l j p k f", p=P)
        down_v = w_down.rearrange("l j (h k p) c -> l j h p k c", p=P, h=2)
        in_v = w_in.rearrange("l (k p) c -> l p k c", p=P)
        out_attn_v = w_out[:, 0:D_ATTN, :].rearrange("l (h j p) c -> l h p j c", h=2, j=4)
        out_conv_v = w_out[:, D_ATTN:D, :].rearrange("l (g k p) c -> l g p k c", p=P, g=2)
        CONV_G, SC_G, ATTN_G = range(3)
        WO = [(SC_G, 0, 4), (ATTN_G, 0, 2), (ATTN_G, 2, 2), (ATTN_G, 4, 2), (CONV_G, 0, 4),
              (SC_G, 4, 4), (CONV_G, 4, 4), (ATTN_G, 6, 2)]
        UNITS_OF = [[i for i in range(KD) if WO[i][1] <= d < WO[i][1] + WO[i][2]] for d in range(KD)]
        COMPLETE = [[d for d in range(KD) if UNITS_OF[d][-1] == i] for i in range(KD)]
        GROUP_TILES = [[4, 5], [6, 7], [0, 1, 2, 3]]
        Y_FIRST = [6, 0, 2]

        @block.sync
        def _(sp):
            for t in range(NT):
                sp.dma_start(xnat[:, t, :], x_in[0, t * P:(t + 1) * P, :]).then_inc(in_landed[t], 16)

            def load(n, s, parts):
                sp.wait_ge(lo_ready, n + 1)
                apart(sp)
                for dst, src in parts:
                    sp.dma_start(dst, src).then_inc(raw_landed[s], 16)

            def ffn(l, j):
                with sp.Fori(0, FT) as f:
                    n = l * UNITS + FFN[j] + 2 * f
                    for s, v in enumerate((gate_v, up_v)):
                        load(n + s, s, [(raw[:, s, 0:KD, :], v[l, j, :, :, bass.ds(f * P, P)])])
                with sp.Fori(0, KD) as d:
                    n = l * UNITS + FFN[j] + DOWN + 2 * d
                    for s in range(2):
                        load(n + s, s, [(raw[:, s, :, :], down_v[l, j, s, :, :, bass.ds(d * P, P)])])

            with sp.Fori(0, L) as l:
                ffn(l, 0)
                for i in range(UT):
                    s = i % 2
                    dst = raw[:, s, 0:KD, :]
                    if COLS[i] is not None:
                        parts = [(dst, in_v[l, :, :, COLS[i]:COLS[i] + P])]
                    else:
                        j = i - UQ
                        parts = [(raw[:, s, 0:KD, h * 64:h * 64 + 64],
                                  in_v[l, :, :, (4 * h + j) * 64:(4 * h + j + 1) * 64]) for h in range(2)]
                    load(l * UNITS + W_IN + i, s, parts)
                for i, (g, d0, n) in enumerate(WO):
                    s = i % 2
                    c = slice(d0 * P, (d0 + n) * P)
                    if g == ATTN_G:
                        dst = raw[:, s, 0:KD, :].rearrange("p (j d) c -> p j (d c)", j=4)
                        parts = [(dst[64 * h:64 * h + 64], out_attn_v[l, h, :, :, c]) for h in range(2)]
                    else:
                        dst = raw[:, s, 0:KD, :].rearrange("p (k d) c -> p k (d c)", k=2)
                        parts = [(dst, out_conv_v[l, g, :, :, c])]
                    load(l * UNITS + W_OUT + i, s, parts)
                ffn(l, 1)
            for t in range(NT):
                for h in range(2):
                    sp.wait_ge(y_read[h], t + 1)
                sp.dma_start(out[0, t * P:(t + 1) * P, :], ynat[:, t, :]).then_inc(out_landed, 16)
            sp.wait_ge(out_landed, 16 * NT)

        def extra(n):
            more = [0, 0]
            for m in range(n % 2, n + 1, 2):
                if W_IN + UQ <= m < W_IN + UQ + 4:
                    more[m % 2] += 16
                if W_OUT <= m < W_OUT + KD and WO[m - W_OUT][0] == ATTN_G:
                    more[m % 2] += 16
            return more[n % 2]

        PER_SLOT = [16 * UNITS // 2 + extra(UNITS - 2 + s) for s in range(2)]

        def next_layer(l, more):
            return [[(l + 1, 2 * h + k) for k in range(2)] if more else [] for h in range(2)]

        @block.gpsimd
        def _(pool):
            nc.gpsimd.memset(ident[:, :], 0.0).then_inc(ident_zero, 1)
            nc.gpsimd.memset(ones[:, :], 1.0).then_inc(const_ready, 1)
            pool.wait_ge(ident_zero, 1)
            nc.gpsimd.affine_select(out=ident[:, :], in_=ident[:, :], compare_op=ALU.not_equal, fill=1.0,
                                    base=0, pattern=[[-1, P]], channel_multiplier=1).then_inc(const_ready, 1)

            def sum_squares(read, first, count=KD):
                for i in range(count):
                    pool.wait_ge(sq_ready, first + i + 1)
                    if i == 0:
                        if read is not None:
                            pool.wait_ge(stat_ready, read)
                            apart(pool)
                        nc.gpsimd.tensor_copy(acc[:, :], sq[:, i % 2, :]).then_inc(acc_ready, 1)
                    else:
                        pool.wait_ge(acc_ready, first + i)
                        nc.gpsimd.tensor_tensor(acc[:, :], acc[:, :], sq[:, i % 2, :], ALU.add)\
                            .then_inc(acc_ready, 1)

            sum_squares(None, 0)
            with nc.gpsimd.Fori(0, L) as l:
                r, n = KD + l * RESES, l * NORMS
                sum_squares(n + NORM_FFN0 + 1, r + RES[0])
                pool.wait_ge(x_ready, r + RES[1])
                apart(pool)
                nc.gpsimd.memset(z[:, :, 0:TAPS - 1], 0.0)
                nc.gpsimd.memset(cx[:, :, 0:SC_TAPS - 1], 0.0)
                nc.gpsimd.memset(probs[:, :, 0:2, CHUNK:P], 0.0).then_inc(pads_zero, 1)
                for p in range(PAIRS):
                    sqa = gate[:, :].rearrange("p (c j q) -> p j c q", c=2, j=4)
                    to = prod[:, p * P:(p + 1) * P].rearrange("p (c q) -> p c q", c=2)
                    pool.wait_ge(sqa_ready, l * PAIRS + p + 1)
                    for j in range(1, 4):
                        if j > 1:
                            pool.wait_ge(sqa_sum, l * 3 * PAIRS + 3 * p + j - 1)
                        nc.gpsimd.tensor_tensor(to, sqa[:, 0] if j == 1 else to, sqa[:, j], ALU.add)\
                            .then_inc(sqa_sum, 1)
                sum_squares(n + NORM_MIX + 1, r + RES[1])
                sum_squares(n + NORM_FFN1 + 1, r + RES[2])

        @block.scalar
        def _(act):
            loads = [(parnat[C_NORM:C_NORM + 3 * L * KD, :], g_norm.rearrange("l i (k p) -> (l i k) p", p=P)),
                     (parnat[C_NORM + 3 * L * KD:C_GRP, :], g_final.rearrange("(k p) -> k p", p=P)),
                     (parnat[C_BDW:C_GLN, :], b_dw31.rearrange("l (c p) -> (l c) p", p=P)),
                     (parnat[C_GLN:C_BLN, :], g_ln.rearrange("l (c p) -> (l c) p", p=P)),
                     (parnat[C_BLN:C_SC3, :], b_ln.rearrange("l (c p) -> (l c) p", p=P)),
                     (parnat[C_SC3:N_PAR, :], w_sc3.rearrange("l t (c p) -> (l t c) p", p=P)),
                     (dwnat[0:N_DW, :], w_dw31.rearrange("l t (c p) -> (l t c) p", p=P)),
                     (sinknat[:, :], sinks.rearrange("(o l) h -> o (l h)", o=1).to_broadcast([P, L * HEADS]))]
            for l in range(L):
                c = C_GRP + l * KD
                for h in range(2):
                    loads.append((parnat[c:c + 4, 64 * h:64 * h + 64],
                                  g_grp[l, 256 * h:256 * h + 256].rearrange("(j q) -> j q", q=64)))
                loads.append((parnat[c + 4:c + KD, :], g_grp[l, D_ATTN:D].rearrange("(k p) -> k p", p=P)))
            for i, (dst, src) in enumerate(loads):
                act.dma_start(dst, src).then_inc(gains_landed if i == 0 else par_landed, 16)
            assert len(loads) == PAR_LOADS + 1

            def split(l, numbers, tiles):
                n, s, landed = numbers
                act.wait_ge(raw_landed[s % 2], landed)
                act.wait_ge(unit_done, l * UNITS + n + 1)
                nc.scalar.copy(wh[:, s % RING, 0:tiles, :], raw[:, s % RAW, 0:tiles, :]).then_inc(hi_ready, 1)

            def unit(l, n):
                return n, n, l * PER_SLOT[n % 2] + 16 * (n // 2 + 1) + extra(n)

            def loop_unit(l, n0, i, k):
                return n0 + 4 * i + k, k, l * PER_SLOT[k % 2] + 16 * (n0 // 2 + k // 2 + 1) + extra(n0 + k) + 32 * i

            def squares(n, parity, src):
                if not (isinstance(n, int) and n < 2):
                    act.wait_ge(acc_ready, n - 1)
                    apart(act)
                nc.scalar.activation(sq[:, parity, :], src, ACT.Square).then_inc(sq_ready, 1)

            def root(stream, n, features, eps=RMS_EPS):
                stat_s, root_s, _, _, _, _, k, b = stream
                act.wait_ge(stat_s, n + 1)
                nc.scalar.activation(small[:, k, 0, :], bank[b][:, 0:NT], ACT.Sqrt, bias=eps,
                                     scale=1.0 / features).then_inc(root_s, 1)

            def rsqrt_diagonal(stream, n):
                _, _, inv_s, diag_s, _, to, k, _ = stream
                act.wait_ge(inv_s, n + 1)
                for t in range(NT):
                    d = nc.scalar.activation(to[:, t * P:(t + 1) * P], ident[:, :], ACT.Copy,
                                             scale=small[:, k, 1, t:t + 1])
                d.then_inc(diag_s, 1)

            def rsqrt(n, features=D):
                root(NORM_A, n, features)
                rsqrt_diagonal(NORM_A, n)
                act.wait_ge(spread_ready, n + 1)
                nc.scalar.copy(rstd[:, :], bank[STAT][:, :]).then_inc(rstd_ready, 1)

            def chunked(ap, t):
                return ap.rearrange("p (n q) -> p n q", q=CHUNK) if UQ <= t < UQ + 4 else ap

            def tile(t):
                return uq[:, :, t - UQ, :] if UQ <= t < UQ + 4 else u[:, t, :]

            act.wait_ge(par_t, 1)
            nc.scalar.copy(par[:, 0:GAINS], bank[STAT][:, 0:GAINS]).then_inc(par_ready, 1)
            act.wait_ge(par_ready, 1)
            for d in range(KD):
                act.wait_ge(x_ready, d + 1)
                nc.scalar.activation(xh[:, d, :], x[:, d, :], ACT.Copy, scale=par[:, C_NORM + d:C_NORM + d + 1])\
                    .then_inc(xh_ready, 1)
                squares(d, d % 2, x[:, d, :])
                if d == 0:
                    split(0, unit(0, 0), KD)
            for n in range(1, 4):
                split(0, unit(0, n), KD)
            act.wait_ge(par_t, 3)
            nc.scalar.copy(par[:, GAINS:N_PAR], bank[HEADS_OUT][:, GAINS:N_PAR])
            nc.scalar.copy(dw[:, :], bank[HEADS_OUT][:, P:P + N_DW]).then_inc(par_ready, 1)
            act.wait_ge(par_ready, 2)

            def ffn(l, j, last_ahead, last=False):
                base = FFN[j]

                def hidden(f, a, b):
                    F = (2 * l + j) * FT + f
                    act.wait_ge(gate_ready, F + 1)
                    nc.scalar.activation(gate[:, :], gate[:, :], ACT.Silu).then_inc(silu_ready, 1)
                    for n, tiles in (a, b):
                        split(l, n, tiles)
                    act.wait_ge(prod_ready, F + 1)
                    apart(act)
                    at_f = acth[:, f, :] if isinstance(f, int) else acth[:, bass.ds(f, 1), :].rearrange("p a t -> p (a t)")
                    nc.scalar.copy(at_f, prod[:, :]).then_inc(acth_ready, 1)

                rsqrt(l * NORMS + (NORM_FFN0, NORM_FFN1)[j])
                for f in range(2):
                    hidden(f, *[(unit(l, base + 4 + 2 * f + k), KD) for k in range(2)])
                with nc.scalar.Fori(1, FT // 2 - 1) as i:
                    for h in range(2):
                        hidden(2 * i + h, *[(loop_unit(l, base + 4, i, 2 * h + k), KD) for k in range(2)])
                for h in range(2):
                    f = FT - 2 + h
                    hidden(f, *[(unit(l, base + DOWN + 2 * h + k), HALF) for k in range(2)])

                def residual(d, h):
                    r = KD + l * RESES + RES[2 * j] + d
                    c = C_NORM + l * 3 * KD + (2 * j + 1) * KD + d
                    act.wait_ge(x_ready, r + 1)
                    apart(act)
                    xd, xhd = (t[:, bass.ds(d, 1), :].rearrange("p a t -> p (a t)") for t in (x, xh))
                    if not last:
                        nc.scalar.activation(xhd, xd, ACT.Copy, scale=par[:, bass.ds(c, 1)]).then_inc(xh_ready, 1)
                    squares(r, h, xd)

                with nc.scalar.Fori(0, KD // 2 - 1) as i:
                    for h in range(2):
                        residual(2 * i + h, h)
                        for k in range(2):
                            split(l, loop_unit(l, base + DOWN + 4, i, 2 * h + k), HALF)
                for h in range(2):
                    residual(KD - 2 + h, h)
                    for layer_of, n in last_ahead[h]:
                        split(layer_of, unit(layer_of, n), KD)

            def layer(l, more):
                ffn(l, 0, [[(l, W_IN + 2 * h + k) for k in range(2)] for h in range(2)])

                rsqrt(l * NORMS + NORM_MIX)
                for m in range(CT):
                    split(l, unit(l, W_IN + 4 + 2 * m), KD)
                    act.wait_ge(proj_read, l * PROJS + PROJ[1] + 2 * m + 2 + 4)
                    nc.scalar.activation(u[:, CG[m], :], u[:, CG[m], :], ACT.Sigmoid).then_inc(sig_ready, 1)
                    split(l, unit(l, W_IN + 5 + 2 * m), KD)
                    act.wait_ge(gated, l * CT + m + 1)
                    apart(act)
                    nc.scalar.activation(u[:, CA[m], :], z[:, m, 0:T], ACT.Identity,
                                         scale=dw[:, bass.ds(l * TAPS * CT + m, 1)],
                                         bias=par[:, bass.ds(l * CT + C_BDW + m, 1)]).then_inc(first_tap, 1)
                for i in range(4, 10):
                    split(l, unit(l, W_IN + 4 + i), KD)

                def exps(p):
                    act.wait_ge(max_ready, l * PAIRS + p + 1)
                    if p:
                        act.wait_ge(probsT_ready, 2 * (l * PAIRS + p))
                    for kv in range(2):
                        for g in range(4):
                            keys = CHUNK if p == 0 and g < 2 else P
                            i = 4 * kv + g
                            nc.scalar.activation(probs[:, kv, g, 0:keys], bank[SCORES + kv][:, g * P:g * P + keys],
                                                 ACT.Exp, bias=soft[:, S_NEG, p, i:i + 1], scale=HEAD_DIM ** -0.5,
                                                 accum_out=soft[:, S_SUM, p, i:i + 1])
                    nc.scalar.activation(soft[:, S_ES, p, :], soft[:, S_SINK, p, :], ACT.Exp).then_inc(exp_ready, 1)

                def normalise(p):
                    act.wait_ge(den_ready, l * PAIRS + p + 1)
                    for i in range(8):
                        pr = probs[:, i // 4, i % 4, :]
                        t = nc.scalar.activation(pr, pr, ACT.Copy, scale=soft[:, S_R, p, i:i + 1])
                    t.then_inc(probs_ready, 1)

                def copy_probsT(p):
                    for kv in range(2):
                        act.wait_ge(probsT_ready, 2 * (l * PAIRS + p) + kv + 1)
                        if p:
                            act.wait_ge(o_ready, l * PAIRS + p)
                        nc.scalar.copy(probsT[:, kv, :, :].rearrange("p g q -> p (g q)"), bank[PROBS_T + kv][:, :])\
                            .then_inc(probsT_read, 1)

                def heads_squares(p):
                    act.wait_ge(o_read, l * PAIRS + p + 1)
                    if p:
                        act.wait_ge(sqa_sum, 3 * (l * PAIRS + p))
                    nc.scalar.activation(gate[:, :], uq[:, 2 * p:2 * p + 2, :, :].rearrange("p c j q -> p (c j q)"),
                                         ACT.Square).then_inc(sqa_ready, 1)

                def squares_b(norm, c, src):
                    if norm:
                        act.wait_ge(statb_ready, l * NORMS_B + norm)
                    elif c == 0:
                        act.wait_ge(acc_ready, KD + l * RESES + RES[1])
                    nc.scalar.activation(sq[:, c, :], src, ACT.Square).then_inc(sqb_ready, 1)

                def root_b(norm, eps=RMS_EPS):
                    root(NORM_B, l * NORMS_B + norm, D_CONV, eps)

                def diagonal_b(norm):
                    rsqrt_diagonal(NORM_B, l * NORMS_B + norm)

                def read_heads(p):
                    act.wait_ge(o_ready, l * PAIRS + p + 1)
                    nc.scalar.copy(uq[:, 2 * p:2 * p + 2, :, :].rearrange("p c j q -> p (c j q)"),
                                   bank[HEADS_OUT][:, :]).then_inc(o_read, 1)
                    heads_squares(p)

                def high_y(tiles, y0, ready0):
                    for i, t in enumerate(tiles):
                        act.wait_ge(y_ready, l * KD + ready0 + i + 1)
                        nc.scalar.copy(chunked(yh[:, y0 + i, :], t), tile(t)).then_inc(yh_ready, 1)

                exps(0)
                normalise(0)
                for b in range(2):
                    act.wait_ge(v_t, 2 * l + b + 1)
                    nc.scalar.copy(vtok[:, 4 * b:4 * b + 4, :].rearrange("p n d -> p (n d)"), bank[PROBS_T + b][:, :])\
                        .then_inc(v_ready, 1)
                split(l, unit(l, W_IN + 14), KD)
                copy_probsT(0)
                exps(1)
                normalise(1)
                split(l, unit(l, W_IN + 15), KD)
                read_heads(0)
                split(l, unit(l, W_OUT + 0), KD)
                copy_probsT(1)
                exps(2)
                normalise(2)
                split(l, unit(l, W_OUT + 1), KD)
                read_heads(1)
                copy_probsT(2)
                exps(3)
                read_heads(2)
                split(l, unit(l, W_OUT + 2), KD)
                normalise(3)
                copy_probsT(3)
                for c in range(CT):
                    act.wait_ge(sc_ready, l * CT + c + 1)
                    squares_b(NORM_SC, c, u[:, SB[c], :])
                read_heads(3)
                root_b(NORM_SC)
                diagonal_b(NORM_SC)
                root(NORM_O, l * NORMS + NORM_ATTN, D_ATTN)
                rsqrt_diagonal(NORM_O, l * NORMS + NORM_ATTN)
                high_y(SB, 6, Y_FIRST[SC_G])
                split(l, unit(l, W_OUT + 3), KD)
                high_y([UQ + i for i in range(2)], 0, Y_FIRST[ATTN_G])
                for c in range(CT):
                    act.wait_ge(ln_ready, l * 2 * CT + c + 1)
                    squares_b(NORM_LN, c, u[:, CA[c], :])
                high_y([UQ + i for i in range(2, 4)], 2, Y_FIRST[ATTN_G] + 2)
                root_b(NORM_LN, LN_EPS)
                diagonal_b(NORM_LN)
                for c in range(CT):
                    act.wait_ge(ln_ready, l * 2 * CT + CT + c + 1)
                    apart(act)
                    nc.scalar.activation(u[:, CA[c], :], u[:, CA[c], :], ACT.Silu,
                                         bias=par[:, bass.ds(l * CT + C_BLN + c, 1)],
                                         scale=par[:, bass.ds(l * CT + C_GLN + c, 1)]).then_inc(silu_conv, 1)
                for c in range(CT):
                    act.wait_ge(silu_conv, l * CT + c + 1)
                    squares_b(NORM_CONV, c, u[:, CA[c], :])
                root_b(NORM_CONV)
                diagonal_b(NORM_CONV)
                high_y(CA, 4, Y_FIRST[CONV_G])

                for i in range(KD):
                    for d in COMPLETE[i]:
                        r = KD + l * RESES + RES[1] + d
                        act.wait_ge(x_ready, r + 1)
                        apart(act)
                        nc.scalar.activation(xh[:, d, :], x[:, d, :], ACT.Copy,
                                             scale=par[:, bass.ds(l * 3 * KD + C_NORM + 2 * KD + d, 1)])\
                            .then_inc(xh_ready, 1)
                        if d < 2:
                            act.wait_ge(statb_ready, l * NORMS_B + NORMS_B)
                            nc.scalar.activation(sq[:, d % 2, :], x[:, d, :], ACT.Square).then_inc(sq_ready, 1)
                        else:
                            squares(r, d % 2, x[:, d, :])
                    split(l, unit(l, W_OUT + 4 + i), KD)
                ffn(l, 1, next_layer(l, more), last=not more)

            with nc.scalar.Fori(0, L - 1) as l:
                layer(l, True)
            layer(L - 1, False)
            root(NORM_A, L * NORMS, D)
            for t in range(NT):
                act.wait_ge(y_t[0], t + 1)
                if t == 0:
                    act.wait_ge(inv_ready, L * NORMS + 1)
                nc.scalar.activation(ynat[:, t, 0:T], bank[2 * (t % 2)][:, :], ACT.Copy, scale=small[:, 0, 1, t:t + 1])\
                    .then_inc(y_read[0], 1)

        @block.vector
        def _(dve):
            dve.sem_inc(lo_ready, RAW)
            dve.sem_inc(proj_read, 4)

            def split(l, n, s, tiles):
                dve.wait_ge(hi_ready, l * UNITS + n + 1)
                nc.vector.tensor_tensor(wl[:, s % RING, 0:tiles, :], raw[:, s % RAW, 0:tiles, :],
                                        wh[:, s % RING, 0:tiles, :].bitcast(F32), ALU.subtract)\
                    .then_inc(lo_ready, 1)

            def low_x(cnt, d, column):
                xd, hd, ld = (t[:, d, :] if isinstance(d, int) else t[:, bass.ds(d, 1), :].rearrange("p a t -> p (a t)")
                              for t in (x, xh, xl))
                dve.wait_ge(xh_ready, cnt + 1)
                nc.vector.scalar_tensor_tensor(out=ld, in0=xd, scalar=column, in1=hd.bitcast(F32),
                                               op0=ALU.mult, op1=ALU.subtract).then_inc(xl_ready, 1)

            def inverse(stream, n):
                _, root_s, inv_s, _, _, _, k, _ = stream
                dve.wait_ge(root_s, n + 1)
                nc.vector.reciprocal(small[:, k, 1, :], small[:, k, 0, :]).then_inc(inv_s, 1)

            for d in range(KD + 2):
                if d < KD:
                    dve.wait_ge(in_t, d + 1)
                    nc.vector.tensor_copy(x[:, d, :], bank[X_BANKS[d]][:, :]).then_inc(x_ready, 1)
                if d == 2:
                    dve.wait_ge(par_ready, 1)
                if d >= 2:
                    low_x(d - 2, d - 2, par[:, C_NORM + d - 2:C_NORM + d - 1])
                if d == 4:
                    split(0, 0, 0, KD)
            for n in range(1, 4):
                split(0, n, n, KD)
            dve.wait_ge(par_landed, 16 * PAR_LOADS)
            for h in range(2):
                src = sinknat[64 * h:64 * h + 64, :].rearrange("p (c r s) -> p c r s", r=2, s=2)[:, :, :, h]
                to = sink[64 * h:64 * h + 64, :].rearrange("p (c n r) -> p c n r", n=2, r=2)
                for n in range(2):
                    nc.vector.tensor_copy(to[:, :, n, :], src).then_inc(sinks_ready, 1)
            dve.wait_ge(sinks_ready, 4)
            dve.wait_ge(par_ready, 2)

            def ffn(l, j, last_ahead, last=False):
                base = FFN[j]

                def hidden(f, ahead):
                    F = (2 * l + j) * FT + f
                    q = l * PROJS + PROJ[2 * j] + 2 * f
                    n = l * UNITS + base + 2 * f + RING
                    b = 2 * (f % 2) if isinstance(f, int) else 2 * ahead[1]
                    dve.wait_ge(unit_done, n + 1)
                    nc.vector.tensor_tensor(gate[:, :], bank[b][:, :], rstd[:, :], ALU.mult).then_inc(gate_ready, 1)
                    dve.wait_ge(unit_done, n + 2)
                    if not (isinstance(f, int) and f == 0):
                        dve.wait_ge(actl_ready, F)
                    nc.vector.tensor_tensor(prod[:, :], bank[b + 1][:, :], rstd[:, :], ALU.mult).then_inc(proj_read, 2)
                    for a, s, tiles in ahead[0]:
                        split(l, a, s, tiles)
                    dve.wait_ge(silu_ready, F + 1)
                    dve.wait_ge(proj_read, q + 6)
                    nc.vector.tensor_tensor(prod[:, :], gate[:, :], prod[:, :], ALU.mult).then_inc(prod_ready, 1)
                    dve.wait_ge(acth_ready, F + 1)
                    hi, lo = (t[:, f, :] if isinstance(f, int) else t[:, bass.ds(f, 1), :].rearrange("p a t -> p (a t)")
                              for t in (acth, actl))
                    nc.vector.tensor_tensor(lo, prod[:, :], hi.bitcast(F32), ALU.subtract).then_inc(actl_ready, 1)

                inverse(NORM_A, l * NORMS + (NORM_FFN0, NORM_FFN1)[j])
                dve.wait_ge(rstd_ready, l * RSTDS + (0, 2)[j] + 1)
                for f in range(2):
                    hidden(f, ([(base + 4 + 2 * f + k, 2 * f + k, KD) for k in range(2)], f))
                with nc.vector.Fori(1, FT // 2 - 1) as i:
                    for h in range(2):
                        hidden(2 * i + h, ([(4 * i + base + 4 + 2 * h + k, 2 * h + k, KD) for k in range(2)], h))
                for h in range(2):
                    hidden(FT - 2 + h, ([(base + DOWN + 2 * h + k, 2 * h + k, HALF) for k in range(2)], h))

                def residual(d, h):
                    r = l * RESES + RES[2 * j] + d
                    dve.wait_ge(unit_done, l * UNITS + base + DOWN + 2 * d + RING + 2)
                    xd = x[:, bass.ds(d, 1), :].rearrange("p a t -> p (a t)")
                    nc.vector.scalar_tensor_tensor(out=xd, in0=bank[RES_BANK + h][:, :], scalar=0.5, in1=xd,
                                                   op0=ALU.mult, op1=ALU.add).then_inc(x_ready, 1)
                    column = par[:, bass.ds(l * 3 * KD + C_NORM + (2 * j + 1) * KD + d, 1)]
                    if last:
                        dve.wait_ge(sq_ready, KD + r + 1)
                        apart(dve)
                        nc.vector.tensor_scalar(xd, xd, column, None, ALU.mult).then_inc(y_scaled, 1)
                    else:
                        low_x(KD + r, d, column)

                with nc.vector.Fori(0, KD // 2 - 1) as i:
                    for h in range(2):
                        residual(2 * i + h, h)
                        for k in range(2):
                            split(l, 4 * i + base + DOWN + 4 + 2 * h + k, 2 * h + k, HALF)
                for h in range(2):
                    residual(KD - 2 + h, h)
                    for layer_of, n in last_ahead[h]:
                        split(layer_of, n, n, KD)

            CONV_STEPS = CT * (TAPS - 1)

            def layer(l, more):
                ffn(l, 0, [[(l, W_IN + 2 * h + k) for k in range(2)] for h in range(2)])

                inverse(NORM_A, l * NORMS + NORM_MIX)
                dve.wait_ge(rstd_ready, l * RSTDS + 2)
                own = [0]

                def step(inst):
                    own[0] += 1
                    inst.then_inc(vec_step, 1)

                def steps_done():
                    dve.wait_ge(vec_step, l * VEC_STEPS + own[0])

                def take(i):
                    dve.wait_ge(unit_done, l * UNITS + W_IN + i + 1 + RING)
                    b = i % 4 if i < TWO_BANKS else i % 2
                    if UQ <= i < UQ + 4:
                        nc.vector.tensor_tensor(uq[:, :, i - UQ, :], chunked(bank[b][:, :], i), chunked(rstd[:, :], i),
                                                ALU.mult).then_inc(proj_read, 1)
                    else:
                        nc.vector.tensor_tensor(u[:, i, :], bank[b][:, :], rstd[:, :], ALU.mult).then_inc(proj_read, 1)

                def taken(i):
                    dve.wait_ge(proj_read, l * PROJS + PROJ[1] + i + 1 + 4)

                def chunked(ap, t):
                    return ap.rearrange("p (n q) -> p n q", q=CHUNK) if UQ <= t < UQ + 4 else ap

                def tile(t):
                    return uq[:, :, t - UQ, :] if UQ <= t < UQ + 4 else u[:, t, :]

                def taps(block):
                    first = 1 + sum(TAP_BLOCKS[:block])
                    count = TAP_BLOCKS[block]

                    def tap(c, t):
                        nc.vector.scalar_tensor_tensor(
                            out=u[:, CA[c], :], in0=z[:, c, bass.ds(t, T)],
                            scalar=dw[:, bass.ds(l * TAPS * CT + CT * t + c, 1)],
                            in1=u[:, CA[c], :], op0=ALU.mult, op1=ALU.add).then_inc(conv_step, 1)

                    if block == 0:
                        for c in range(CT):
                            dve.wait_ge(first_tap, l * CT + c + 1)
                            tap(c, first)
                        first, count = first + 1, count - 1
                    with nc.vector.Fori(0, count) as t:
                        for c in range(CT):
                            dve.wait_ge(conv_step, l * CONV_STEPS + CT * t + CT * (first - 2) + c + 1)
                            tap(c, t + first)

                def maxima(p):
                    dve.wait_ge(scores_ready, l * PAIRS + p + 1)
                    for kv in range(2):
                        sc = bank[SCORES + kv][:, :].rearrange("p (g k) -> p g k", k=P)
                        if p == 0:
                            nc.vector.reduce_max(soft[:, S_MAX, p, 4 * kv:4 * kv + 2], sc[:, 0:2, 0:CHUNK], axis=AX.X)
                            r = nc.vector.reduce_max(soft[:, S_MAX, p, 4 * kv + 2:4 * kv + 4], sc[:, 2:4, :], axis=AX.X)
                        else:
                            r = nc.vector.reduce_max(soft[:, S_MAX, p, 4 * kv:4 * kv + 4], sc, axis=AX.X)
                    step(r)
                    sk = sink[:, bass.ds(l * KV_HEADS * 4, KV_HEADS * 4)]
                    steps_done()
                    step(nc.vector.scalar_tensor_tensor(out=soft[:, S_M, p, :], in0=soft[:, S_MAX, p, :],
                                                        scalar=HEAD_DIM ** -0.5, in1=sk, op0=ALU.mult, op1=ALU.max))
                    steps_done()
                    nc.vector.tensor_scalar(soft[:, S_NEG, p, :], soft[:, S_M, p, :], -1.0, None, ALU.mult)
                    nc.vector.tensor_tensor(soft[:, S_SINK, p, :], sk, soft[:, S_M, p, :], ALU.subtract)\
                        .then_inc(max_ready, 1)

                def invert_sums(p):
                    dve.wait_ge(exp_ready, l * PAIRS + p + 1)
                    step(nc.vector.tensor_tensor(soft[:, S_DEN, p, :], soft[:, S_SUM, p, :], soft[:, S_ES, p, :],
                                                 ALU.add))
                    steps_done()
                    nc.vector.reciprocal(soft[:, S_R, p, :], soft[:, S_DEN, p, :]).then_inc(den_ready, 1)

                def scale_y(tiles, y0, stream, n):
                    dve.wait_ge(stream[4], n + 1)
                    apart(dve)
                    for i, t in enumerate(tiles):
                        nc.vector.scalar_tensor_tensor(out=tile(t), in0=tile(t),
                                                       scalar=par[:, bass.ds(l * KD + C_GRP + y0 + i, 1)],
                                                       in1=chunked(bank[stream[7]][:, :], t), op0=ALU.mult,
                                                       op1=ALU.mult).then_inc(y_ready, 1)

                def low_y(tiles, y0, ready0):
                    for i, t in enumerate(tiles):
                        dve.wait_ge(yh_ready, l * KD + ready0 + i + 1)
                        nc.vector.tensor_tensor(chunked(yl[:, y0 + i, :], t), tile(t),
                                                chunked(yh[:, y0 + i, :].bitcast(F32), t), ALU.subtract)\
                            .then_inc(yl_ready, 1)

                def short_conv(c):
                    a = SC[c]
                    step(nc.vector.tensor_tensor(cx[:, c, SC_TAPS - 1:SC_TAPS - 1 + T], u[:, a, :], u[:, SX[c], :],
                                                 ALU.mult))
                    for t in range(SC_TAPS):
                        steps_done()
                        w = par[:, bass.ds(l * SC_TAPS * CT + C_SC3 + CT * t + c, 1)]
                        if t == 0:
                            step(nc.vector.tensor_scalar(u[:, a, :], cx[:, c, 0:T], w, None, ALU.mult))
                        else:
                            step(nc.vector.scalar_tensor_tensor(out=u[:, a, :], in0=cx[:, c, t:t + T], scalar=w,
                                                                in1=u[:, a, :], op0=ALU.mult, op1=ALU.add))

                def short_conv_gate(c):
                    steps_done()
                    nc.vector.tensor_tensor(u[:, SB[c], :], u[:, SB[c], :], u[:, SC[c], :], ALU.mult)\
                        .then_inc(sc_ready, 1)

                def gated_input(m):
                    dve.wait_ge(sig_ready, l * CT + m + 1)
                    if m == 0:
                        dve.wait_ge(pads_zero, l + 1)
                    nc.vector.tensor_tensor(z[:, m, TAPS - 1:TAPS - 1 + T], u[:, CA[m], :], u[:, CG[m], :], ALU.mult)\
                        .then_inc(gated, 1)

                take(0)
                split(l, W_IN + 4, 0, KD)
                take(1)
                gated_input(0)
                split(l, W_IN + 5, 1, KD)
                take(2)
                split(l, W_IN + 6, 2, KD)
                take(3)
                gated_input(1)
                split(l, W_IN + 7, 3, KD)
                for i in range(4, 9):
                    take(i)
                    split(l, W_IN + 4 + i, i % 4, KD)
                    taps(i - 4)
                take(9)
                taps(5)
                maxima(0)
                split(l, W_IN + 13, 1, KD)
                taps(6)
                invert_sums(0)
                take(10)
                taps(7)
                split(l, W_IN + 14, 2, KD)
                maxima(1)
                taps(8)
                invert_sums(1)
                take(11)
                taps(9)
                split(l, W_IN + 15, 3, KD)
                take(12)
                maxima(2)
                split(l, W_OUT + 0, 0, KD)
                taps(10)
                invert_sums(2)
                short_conv(0)
                short_conv_gate(0)
                take(13)
                split(l, W_OUT + 1, 1, KD)
                maxima(3)
                taps(11)
                take(14)
                invert_sums(3)
                taken(14)
                short_conv(1)
                take(15)
                taken(15)
                short_conv_gate(1)
                taps(12)
                split(l, W_OUT + 2, 2, KD)
                taps(13)
                inverse(NORM_B, l * NORMS_B + NORM_SC)
                taps(14)
                inverse(NORM_O, l * NORMS + NORM_ATTN)
                scale_y(SB, 6, NORM_B, l * NORMS_B + NORM_SC)
                low_y(SB, 6, Y_FIRST[SC_G])
                taps(15)
                scale_y([UQ, UQ + 1], 0, NORM_O, l * NORMS + NORM_ATTN)
                dve.wait_ge(mean_ready, l + 1)
                for c in range(CT):
                    nc.vector.scalar_tensor_tensor(out=u[:, CA[c], :], in0=bank[STAT][:, :], scalar=-1.0 / D_CONV,
                                                   in1=u[:, CA[c], :], op0=ALU.mult, op1=ALU.add).then_inc(ln_ready, 1)
                low_y([UQ], 0, Y_FIRST[ATTN_G])
                scale_y([UQ + 2, UQ + 3], 2, NORM_O, l * NORMS + NORM_ATTN)
                low_y([UQ + 1], 1, Y_FIRST[ATTN_G] + 1)
                low_y([UQ + 2, UQ + 3], 2, Y_FIRST[ATTN_G] + 2)
                inverse(NORM_B, l * NORMS_B + NORM_LN)
                split(l, W_OUT + 3, 3, KD)
                dve.wait_ge(spreadb_ready, l * NORMS_B + NORM_LN + 1)
                for c in range(CT):
                    nc.vector.tensor_tensor(u[:, CA[c], :], u[:, CA[c], :], bank[STAT][:, :], ALU.mult)\
                        .then_inc(ln_ready, 1)
                inverse(NORM_B, l * NORMS_B + NORM_CONV)
                scale_y(CA, 4, NORM_B, l * NORMS_B + NORM_CONV)
                low_y(CA, 4, Y_FIRST[CONV_G])
                assert own[0] == VEC_STEPS

                for i in range(KD):
                    if COMPLETE[i]:
                        dve.wait_ge(unit_done, l * UNITS + W_OUT + i + 1 + RING)
                        for d in COMPLETE[i]:
                            nc.vector.tensor_tensor(x[:, d, :], bank[d][:, :], x[:, d, :], ALU.add).then_inc(x_ready, 1)
                        for d in COMPLETE[i]:
                            low_x(KD + l * RESES + RES[1] + d, d,
                                  par[:, bass.ds(l * 3 * KD + C_NORM + 2 * KD + d, 1)])
                    split(l, W_OUT + 4 + i, i % 4, KD)
                ffn(l, 1, next_layer(l, more), last=not more)

            with nc.vector.Fori(0, L - 1) as l:
                layer(l, True)
            layer(L - 1, False)

            inverse(NORM_A, L * NORMS)
            dve.wait_ge(inv_ready, L * NORMS + 1)
            for t in range(NT):
                dve.wait_ge(y_t[1], t + 1)
                nc.vector.tensor_scalar(ynat[:, t, T:2 * T], bank[2 * (t % 2) + 1][:, :], small[:, 0, 1, t:t + 1], None,
                                        ALU.mult).then_inc(y_read[1], 1)

        @block.tensor
        def _(pe):
            pe.sem_inc(unit_done, RING)

            pe.wait_ge(const_ready, 2)
            pe.wait_ge(gains_landed, 16)
            nc.tensor.transpose(bank[STAT][:, 0:GAINS], parnat[0:GAINS, :], ident[0:GAINS, 0:GAINS]).then_inc(par_t, 1)
            for d in range(KD):
                if d >= 5:
                    pe.wait_ge(x_ready, d - 4)
                for t in range(NT):
                    if d == 0:
                        pe.wait_ge(in_landed[t], 16)
                    mm = nc.tensor.transpose(bank[X_BANKS[d]][:, t * P:(t + 1) * P],
                                             xnat[:, t, d * P:(d + 1) * P], ident[:, :])
                mm.then_inc(in_t, 1)

            pe.wait_ge(par_landed, 16 * PAR_LOADS)
            nc.tensor.transpose(bank[HEADS_OUT][:, 0:N_PAR], parnat[0:N_PAR, :], ident[0:N_PAR, 0:N_PAR])\
                .then_inc(par_t, 1)
            nc.tensor.transpose(bank[HEADS_OUT][:, P:P + N_DW], dwnat[0:N_DW, :], ident[0:N_DW, 0:N_DW])\
                .then_inc(par_t, 1)

            def tile_product(o, s, k, ah, al, first, last):
                nc.tensor.matmul(o, wh[:, s, k, :], ah, start=first, stop=False)
                nc.tensor.matmul(o, wh[:, s, k, :], al, start=False, stop=False)
                return nc.tensor.matmul(o, wl[:, s, k, :], ah, start=False, stop=last)

            def projection(l, n, s, b, reads, done, between={}):
                pe.wait_ge(lo_ready, l * UNITS + n + 1 + RAW)
                pe.wait_ge(proj_read, reads)
                for k in range(KD):
                    pe.wait_ge(xl_ready, done + k + 1)
                    mm = tile_product(bank[b][:, :], s, k, xh[:, k, :], xl[:, k, :], k == 0, k == KD - 1)
                    for small_step in between.get(k, ()):
                        small_step()
                mm.then_inc(unit_done, 1)

            def sum_features(stream, tiles):
                for t in range(NT):
                    for i, tile in enumerate(tiles):
                        mm = nc.tensor.matmul(bank[stream[7]][:, t:t + 1], tile[:, t * P:(t + 1) * P], ones[:, 0:1],
                                              start=i == 0, stop=i == len(tiles) - 1)
                mm.then_inc(stream[0], 1)

            def stat(squares_done):
                pe.wait_ge(acc_ready, squares_done)
                sum_features(NORM_A, [acc])

            def spread(stream, n):
                _, _, _, diag_s, spread_s, src, _, b = stream
                pe.wait_ge(diag_s, n + 1)
                nc.tensor.matmul(bank[b][:, :], ones[:, :], src[:, :], start=True, stop=True).then_inc(spread_s, 1)

            def pair(l, n, q, h, done, between=None):
                for k in range(2):
                    projection(l, n + k, 2 * h + k, 2 * h + k, l * PROJS + q + k + 1, done)
                    if k == 0 and between is not None:
                        between()

            def ffn(l, j):
                base, q0 = FFN[j], PROJ[2 * j]
                done = l * RESES + (0, 2 * KD)[j]
                pair(l, base, q0, 0, done, lambda: stat(done + KD))
                spread(NORM_A, l * NORMS + (NORM_FFN0, NORM_FFN1)[j])
                pair(l, base + 2, q0 + 2, 1, done)
                with nc.tensor.Fori(1, FT // 2) as i:
                    for h in range(2):
                        pair(l, 4 * i + base + 2 * h, 4 * i + q0 + 2 * h, h, done)
                with nc.tensor.Fori(0, KD // 2) as i:
                    for h in range(2):
                        d = 2 * i + h
                        r = l * RESES + RES[2 * j] + d
                        pe.wait_ge(x_ready, r + KD - 1)
                        for k in range(2):
                            s = 2 * h + k
                            pe.wait_ge(lo_ready, l * UNITS + 2 * d + base + DOWN + k + 1 + RAW)
                            for t in range(HALF):
                                f = k * HALF + t
                                pe.wait_ge(actl_ready, (2 * l + j) * FT + f + 1)
                                mm = tile_product(bank[RES_BANK + h][:, :], s, t, acth[:, f, :], actl[:, f, :],
                                                  f == 0, f == FT - 1)
                            mm.then_inc(unit_done, 1)

            with nc.tensor.Fori(0, L) as l:
                ffn(l, 0)
                done = l * RESES + KD
                def take_in(i, between={}):
                    projection(l, W_IN + i, i % 4, i % 4 if i < TWO_BANKS else i % 2,
                               l * PROJS + PROJ[1] + i + 1 + (0 if i < TWO_BANKS else 2), done, between)

                def stat_b(norm):
                    pe.wait_ge(sqb_ready, (l * NORMS_B + norm + 1) * CT)
                    sum_features(NORM_B, [sq[:, c, :] for c in range(CT)])

                def spread_b(norm):
                    spread(NORM_B, l * NORMS_B + norm)

                def scores(p):
                    if p:
                        pe.wait_ge(exp_ready, l * PAIRS + p)
                    for kv in range(2):
                        rows = slice(64 * kv, 64 * kv + 64)
                        for c in range(2):
                            n = 2 * p + c
                            k0 = max(0, (n - 1) * CHUNK)
                            keys = (n + 1) * CHUNK - k0
                            for pr in range(2):
                                g = (2 * c + pr) * P
                                mm = nc.tensor.matmul(
                                    bank[SCORES + kv][:, g:g + keys],
                                    uq[rows, n, 2 * pr:2 * pr + 2, :].rearrange("p j q -> p (j q)"),
                                    u[rows, UK, k0:k0 + keys], start=True, stop=True)
                    mm.then_inc(scores_ready, 1)

                def transpose_probs(p):
                    pe.wait_ge(probs_ready, l * PAIRS + p + 1)
                    if p:
                        pe.wait_ge(probsT_read, 2 * (l * PAIRS + p))
                    else:
                        pe.wait_ge(v_ready, 2 * l + 2)
                    for kv in range(2):
                        for g in range(4):
                            mm = nc.tensor.transpose(bank[PROBS_T + kv][:, g * P:(g + 1) * P], probs[:, kv, g, :],
                                                     ident[:, :])
                        mm.then_inc(probsT_ready, 1)

                def heads(p):
                    if p:
                        pe.wait_ge(o_read, l * PAIRS + p)
                    for kv in range(2):
                        pe.wait_ge(probsT_read, 2 * (l * PAIRS + p) + kv + 1)
                        apart(pe)
                        for c in range(2):
                            n = 2 * p + c
                            K = CHUNK if n == 0 else P
                            mm = nc.tensor.matmul(bank[HEADS_OUT][64 * kv:64 * kv + 64, c * 256:(c + 1) * 256],
                                                  vtok[0:K, n, 64 * kv:64 * kv + 64],
                                                  probsT[0:K, kv, 2 * c:2 * c + 2, :], start=True, stop=True)
                    mm.then_inc(o_ready, 1)

                def project_y(i, between={}):
                    g, d0, n = WO[i]
                    tiles = GROUP_TILES[g]
                    pe.wait_ge(lo_ready, l * UNITS + W_OUT + i + 1 + RAW)
                    for dd in range(n):
                        for k, y in enumerate(tiles):
                            pe.wait_ge(yl_ready, l * KD + Y_FIRST[g] + k + 1)
                            mm = tile_product(bank[d0 + dd][:, :], i % RING, k * n + dd, yh[:, y, :], yl[:, y, :],
                                              i == UNITS_OF[d0 + dd][0] and k == 0,
                                              i == UNITS_OF[d0 + dd][-1] and k == len(tiles) - 1)
                        if dd in between:
                            between[dd]()
                    mm.then_inc(unit_done, 1)

                take_in(0)
                stat(done + KD)
                take_in(1)
                spread(NORM_A, l * NORMS + NORM_MIX)
                for i in range(2, 10):
                    take_in(i)
                pe.wait_ge(proj_read, l * PROJS + PROJ[1] + UV + 4)
                scores(0)
                take_in(10)
                pe.wait_ge(proj_read, l * PROJS + PROJ[1] + UV + 1 + 4)
                for b in range(2):
                    for i in range(4):
                        t0 = max(0, (4 * b + i - 1) * CHUNK)
                        mm = nc.tensor.transpose(bank[PROBS_T + b][:, i * P:(i + 1) * P], u[:, UV, t0:t0 + P],
                                                 ident[:, :])
                    mm.then_inc(v_t, 1)
                take_in(11, {5: [lambda: transpose_probs(0), lambda: scores(1)]})
                heads(0)
                take_in(12)
                transpose_probs(1)
                scores(2)
                take_in(13)
                heads(1)
                take_in(14, {3: [lambda: transpose_probs(2), lambda: scores(3)]})
                heads(2)
                take_in(15)
                transpose_probs(3)
                heads(3)
                pe.wait_ge(rstd_ready, l * RSTDS + 2)
                def stat_attn():
                    pe.wait_ge(sqa_sum, (l + 1) * 3 * PAIRS)
                    pe.wait_ge(o_read, (l + 1) * PAIRS)
                    sum_features(NORM_O, [prod])

                stat_b(NORM_SC)
                stat_attn()
                spread_b(NORM_SC)
                spread(NORM_O, l * NORMS + NORM_ATTN)

                def mean():
                    pe.wait_ge(conv_step, (l + 1) * CONV_STEPS_ALL)
                    pe.wait_ge(y_ready, l * KD + Y_FIRST[SC_G] + CT)
                    for c in range(CT):
                        mm = nc.tensor.matmul(bank[STAT][:, :], ones[:, :], u[:, CA[c], :], start=c == 0,
                                              stop=c == CT - 1)
                    mm.then_inc(mean_ready, 1)

                def stat_ln():
                    pe.wait_ge(ln_ready, l * 2 * CT + CT)
                    stat_b(NORM_LN)

                def stat_conv():
                    pe.wait_ge(ln_ready, (l + 1) * 2 * CT)
                    stat_b(NORM_CONV)

                pe.wait_ge(proj_read, l * PROJS + PROJ[2] + 4)
                pe.wait_ge(exp_ready, (l + 1) * PAIRS)
                project_y(0, {1: mean})
                stat_ln()
                project_y(1, {0: lambda: spread_b(NORM_LN)})
                project_y(2, {0: stat_conv, 1: lambda: spread_b(NORM_CONV)})
                project_y(3)
                for i in range(4, KD):
                    project_y(i)
                ffn(l, 1)

            def tokens(t, h):
                if t >= 2:
                    pe.wait_ge(y_read[h], t - 1)
                for k in range(4 * h, 4 * h + 4):
                    pe.wait_ge(y_scaled, k + 1)
                    mm = nc.tensor.transpose(bank[2 * (t % 2) + h][:, k % 4 * P:(k % 4 + 1) * P],
                                             x[:, k, t * P:(t + 1) * P], ident[:, :])
                mm.then_inc(y_t[h], 1)

            for h in range(2):
                for t in range(2):
                    tokens(t, h)
            stat(L * RESES + KD)
            for t in range(2, NT):
                for h in range(2):
                    tokens(t, h)


PAR_LOADS = 13
CONV_STEPS_ALL = 2 * 30
VEC_STEPS = 3 * 4 + 2 * 4


_INS = ["x", "g_norm", "w_ff_gate", "w_ff_up", "w_ff_down", "w_in", "w_dw31", "b_dw31",
        "g_ln_conv", "b_ln_conv", "w_sc3", "sinks", "g_grp", "w_out", "g_final"]


def kernel(**inputs):
    import numpy as _np
    import concourse.bacc as _bacc
    from concourse import mybir as _mybir
    from concourse.bass_utils import run_bass_kernel_spmd as _run

    nc = _bacc.Bacc("TRN2", target_bir_lowering=False, num_devices=1)
    arrays, args = {}, []
    for name in _INS:
        a = _np.ascontiguousarray(inputs[name])
        arrays[f"in_{name}_dram"] = a
        args.append(nc.dram_tensor(f"in_{name}_dram", a.shape, _mybir.dt.from_np(a.dtype), kind="ExternalInput").ap())
    shape = inputs["x"].shape
    args.append(nc.dram_tensor("out_dram", shape, _mybir.dt.float32, kind="ExternalOutput").ap())
    encoder_trunk(nc, *args)
    r = _run(nc, [arrays], core_ids=[0])
    return r.results[0]["out_dram"]
```
